# Optimizing a Trainium2 kernel written in Bass

```python
import math
import jax, jax.numpy as jnp
from jax import lax
import numpy as np

D_MODEL = 2048
BATCH = 1
SEQ = 256
DEPTH = 2

HEAD_DIM = 128
N_MIX_HEADS = D_MODEL // HEAD_DIM
A_HEADS = 3 * N_MIX_HEADS // 4
A_WIDTH = A_HEADS * HEAD_DIM
B_GROUPS = N_MIX_HEADS - A_HEADS
B_GROUP_DIM = HEAD_DIM
B_WIDTH = B_GROUPS * B_GROUP_DIM
EVEN_IN_WIDTH = 3 * A_WIDTH + B_WIDTH
DILATED_CONFIGS = ((128, 1), (512, 4), (2048, 16))
C_HEADS = D_MODEL // (2 * HEAD_DIM)
C_QK_WIDTH = C_HEADS * 2 * HEAD_DIM
C_V_DIM = 2 * HEAD_DIM
ODD_IN_WIDTH = 2 * C_QK_WIDTH + C_HEADS * C_V_DIM
D_FF = 4 * D_MODEL
NUM_BUCKETS = 32
MAX_DISTANCE = 1024
BIAS_HEADS = A_HEADS + C_HEADS
Q_BLOCK = 128
NORM_EPS = 1e-6
NEG_INF = -1e30
N_EVEN = (DEPTH + 1) // 2
N_ODD = DEPTH // 2

kernel_name = "hybrid_dilated_fourier_diffattn_encoder"

def rmsnorm(x, g):
    xf = x.astype(jnp.float32)
    y = xf * lax.rsqrt(jnp.mean(xf * xf, axis=-1, keepdims=True) + NORM_EPS)
    return (y * g.astype(jnp.float32)).astype(x.dtype)

def t5_bucket(rel):
    half = NUM_BUCKETS // 2
    base = jnp.where(rel > 0, half, 0)
    n = jnp.abs(rel)
    max_exact = half // 2
    nf = jnp.maximum(n, 1).astype(jnp.float32)
    large = max_exact + (jnp.log(nf / max_exact) / math.log(MAX_DISTANCE / max_exact)
                         * (half - max_exact)).astype(jnp.int32)
    large = jnp.minimum(large, half - 1)
    return base + jnp.where(n < max_exact, n, large)

def dilated_branch(q, k, v, table_a, window, dil):
    B, S, H, Dh = q.shape
    half = window // (2 * dil)
    qb = half
    L = S // dil
    nb = -(-L // qb)
    Lp = nb * qb

    def to_cls(t):
        t = t.reshape(B, L, dil, H, Dh).transpose(0, 2, 1, 3, 4)
        return jnp.pad(t, ((0, 0), (0, 0), (0, Lp - L), (0, 0), (0, 0)))

    def band(t):
        tp = jnp.pad(t, ((0, 0), (0, 0), (qb, qb), (0, 0), (0, 0)))
        tp = tp.reshape(B, dil, nb + 2, qb, H, Dh)
        return jnp.concatenate([tp[:, :, :-2], tp[:, :, 1:-1], tp[:, :, 2:]], axis=3)

    qblk = to_cls(q).reshape(B, dil, nb, qb, H, Dh)
    kband = band(to_cls(k))
    vband = band(to_cls(v)).astype(jnp.float32)

    qi = jnp.arange(qb)
    kj = jnp.arange(3 * qb)
    rel = kj[None, :] - qb - qi[:, None]
    t_key = jnp.arange(nb)[:, None] * qb + kj[None, :] - qb
    key_ok = (t_key >= 0) & (t_key < L)
    mask = (jnp.abs(rel) <= half)[None] & key_ok[:, None, :]
    bias = table_a.astype(jnp.float32)[t5_bucket(rel * dil)].transpose(2, 0, 1)

    logits = jnp.einsum('bcnqhd,bcnkhd->bcnhqk', qblk, kband).astype(jnp.float32)
    logits = logits * (1.0 / math.sqrt(Dh)) + bias[None, None, None]
    logits = jnp.where(mask[None, None, :, None], logits, NEG_INF)
    m = jnp.max(logits, axis=-1, keepdims=True)
    p = jnp.exp(logits - m)
    den = jnp.sum(p, axis=-1)
    o = jnp.einsum('bcnhqk,bcnkhd->bcnqhd', p, vband)
    o = o / den.transpose(0, 1, 2, 4, 3)[..., None]
    lse = (m[..., 0] + jnp.log(den)).transpose(0, 1, 2, 4, 3)

    o = o.reshape(B, dil, Lp, H, Dh)[:, :, :L].transpose(0, 2, 1, 3, 4).reshape(B, S, H, Dh)
    lse = lse.reshape(B, dil, Lp, H)[:, :, :L].transpose(0, 2, 1, 3).reshape(B, S, H)
    return o, lse

def dilated_attention(q, k, v, table_a):
    outs, lses = [], []
    for window, dil in DILATED_CONFIGS:
        o, l = dilated_branch(q, k, v, table_a, window, dil)
        outs.append(o)
        lses.append(l)
    w = jax.nn.softmax(jnp.stack(lses, axis=0), axis=0)
    return jnp.sum(w[..., None] * jnp.stack(outs, axis=0), axis=0)

def fourier_mix(u, w_f):
    B, S, _ = u.shape
    g = u.reshape(B, S, B_GROUPS, B_GROUP_DIM).astype(jnp.float32)
    f = jnp.fft.fft2(g, axes=(1, 3), norm='ortho').real
    return jnp.einsum('bsgc,gce->bsge', f, w_f.astype(jnp.float32)).reshape(B, S, B_WIDTH)

def even_mixer(h, w_in, w_f, w_out, table):
    B, S, _ = h.shape
    proj = h @ w_in
    qa = proj[..., :A_WIDTH].reshape(B, S, A_HEADS, HEAD_DIM)
    ka = proj[..., A_WIDTH:2 * A_WIDTH].reshape(B, S, A_HEADS, HEAD_DIM)
    va = proj[..., 2 * A_WIDTH:3 * A_WIDTH].reshape(B, S, A_HEADS, HEAD_DIM)
    ub = proj[..., 3 * A_WIDTH:]
    oa = dilated_attention(qa, ka, va, table[:, :A_HEADS]).reshape(B, S, A_WIDTH)
    ob = fourier_mix(ub, w_f)
    return jnp.concatenate([oa, ob], axis=-1).astype(h.dtype) @ w_out

def diff_attention(h, w_qkv, w_out, lq1, lk1, lq2, lk2, subln_g, table, layer_idx):
    B, S, _ = h.shape
    lambda_init = 0.8 - 0.6 * math.exp(-0.3 * layer_idx)
    proj = h @ w_qkv
    q = proj[..., :C_QK_WIDTH].reshape(B, S, C_HEADS, 2, HEAD_DIM)
    k = proj[..., C_QK_WIDTH:2 * C_QK_WIDTH].reshape(B, S, C_HEADS, 2, HEAD_DIM)
    v = proj[..., 2 * C_QK_WIDTH:].reshape(B, S, C_HEADS, C_V_DIM).astype(jnp.float32)
    f32 = jnp.float32
    lam = (jnp.exp(jnp.sum(lq1.astype(f32) * lk1.astype(f32)))
           - jnp.exp(jnp.sum(lq2.astype(f32) * lk2.astype(f32))) + lambda_init)
    table_c = table[:, A_HEADS:].astype(f32)
    nqb = S // Q_BLOCK
    qblocks = jnp.moveaxis(q.reshape(B, nqb, Q_BLOCK, C_HEADS, 2, HEAD_DIM), 1, 0)
    kpos = jnp.arange(S)
    scale = 1.0 / math.sqrt(HEAD_DIM)

    def one_block(args):
        qb, i = args
        qpos = i * Q_BLOCK + jnp.arange(Q_BLOCK)
        rel = kpos[None, :] - qpos[:, None]
        bias = table_c[t5_bucket(rel)].transpose(2, 0, 1)
        logits = jnp.einsum('bqhcd,bkhcd->bhcqk', qb, k).astype(f32) * scale
        p = jax.nn.softmax(logits + bias[None, :, None], axis=-1)
        a = p[:, :, 0] - lam * p[:, :, 1]
        return jnp.einsum('bhqk,bkhe->bqhe', a, v)

    o = lax.map(one_block, (qblocks, jnp.arange(nqb)))
    o = jnp.moveaxis(o, 0, 1).reshape(B, S, C_HEADS, C_V_DIM)
    o = rmsnorm(o, subln_g) * (1.0 - lambda_init)
    return o.reshape(B, S, C_HEADS * C_V_DIM).astype(h.dtype) @ w_out

def sqrelu_mlp(h, w1, w2):
    return jnp.square(jax.nn.relu(h @ w1)) @ w2

def setup_inputs(seed: int = 0) -> dict:
    key = jax.random.key(seed)
    ks = jax.random.split(key, 20)
    f32 = jnp.float32
    nrm = lambda k, shape, s: jax.random.normal(k, shape, f32) * s
    return {
        'x': nrm(ks[0], (BATCH, SEQ, D_MODEL), 1.0),
        'norm_mix_g': 1.0 + nrm(ks[1], (DEPTH, D_MODEL), 0.02),
        'norm_ffn_g': 1.0 + nrm(ks[2], (DEPTH, D_MODEL), 0.02),
        'norm_final_g': 1.0 + nrm(ks[3], (D_MODEL,), 0.02),
        'rel_bias_table': nrm(ks[4], (NUM_BUCKETS, BIAS_HEADS), 0.3),
        'w_in_even': nrm(ks[5], (N_EVEN, D_MODEL, EVEN_IN_WIDTH), D_MODEL ** -0.5),
        'w_fnet': nrm(ks[6], (N_EVEN, B_GROUPS, B_GROUP_DIM, B_GROUP_DIM), B_GROUP_DIM ** -0.5),
        'w_out_even': nrm(ks[7], (N_EVEN, D_MODEL, D_MODEL), D_MODEL ** -0.5),
        'w_qkv_odd': nrm(ks[8], (N_ODD, D_MODEL, ODD_IN_WIDTH), D_MODEL ** -0.5),
        'lambda_q1': nrm(ks[9], (N_ODD, HEAD_DIM), 0.1),
        'lambda_k1': nrm(ks[10], (N_ODD, HEAD_DIM), 0.1),
        'lambda_q2': nrm(ks[11], (N_ODD, HEAD_DIM), 0.1),
        'lambda_k2': nrm(ks[12], (N_ODD, HEAD_DIM), 0.1),
        'subln_g': 1.0 + nrm(ks[13], (N_ODD, C_V_DIM), 0.02),
        'w_out_odd': nrm(ks[14], (N_ODD, D_MODEL, D_MODEL), D_MODEL ** -0.5),
        'w_ff1': nrm(ks[15], (DEPTH, D_MODEL, D_FF), D_MODEL ** -0.5),
        'w_ff2': nrm(ks[16], (DEPTH, D_FF, D_MODEL), 0.5 * D_FF ** -0.5),
    }

def reference(x, norm_mix_g, norm_ffn_g, norm_final_g, rel_bias_table, w_in_even, w_fnet,
              w_out_even, w_qkv_odd, lambda_q1, lambda_k1, lambda_q2, lambda_k2, subln_g,
              w_out_odd, w_ff1, w_ff2):
    for i in range(DEPTH):
        h = rmsnorm(x, norm_mix_g[i])
        j = i // 2
        if i % 2 == 0:
            x = x + even_mixer(h, w_in_even[j], w_fnet[j], w_out_even[j], rel_bias_table)
        else:
            x = x + diff_attention(h, w_qkv_odd[j], w_out_odd[j], lambda_q1[j], lambda_k1[j],
                                   lambda_q2[j], lambda_k2[j], subln_g[j], rel_bias_table, i)
        x = x + sqrelu_mlp(rmsnorm(x, norm_ffn_g[i]), w_ff1[i], w_ff2[i])
    return rmsnorm(x, norm_final_g)


_drawn_inputs = setup_inputs


def setup_inputs(seed=0):
    import zlib

    import numpy as np

    out = dict(_drawn_inputs(seed))
    spreads = {}
    factors = {'norm_mix_g': 3.287,
     'norm_ffn_g': 3.589,
     'norm_final_g': 8.68,
     'lambda_q1': 3.092,
     'subln_g': 35.814,
     'lambda_q2': 3.531}
    for name, (base, spread) in spreads.items():
        noise = np.random.default_rng([zlib.crc32(name.encode()), seed]).standard_normal(out[name].shape)
        drawn = base * np.exp(spread * noise) if base else spread * noise
        out[name] = __import__('jax').numpy.asarray(drawn.astype(out[name].dtype))
    for name, factor in factors.items():
        out[name] = (out[name] * factor).astype(out[name].dtype)
    return out
```

```python
from contextlib import ExitStack
import math

import numpy as np
import concourse.bass as bass
from concourse import mybir

F32 = mybir.dt.float32
F32R = mybir.dt.float32r
ALU = mybir.AluOpType
ACT = mybir.ActivationFunctionType
AX_X = mybir.AxisListType.X

P = 128
D = 2048
SEQ = 256
KT = D // P
QT = SEQ // P
A_HEADS, GROUPS, C_HEADS = 12, 4, 8
HEADS = A_HEADS + C_HEADS
BUCKETS = 32
FF_CHUNKS = 4
EPS = 1e-6
SCALE = 1.0 / math.sqrt(P)
LAMBDA_INIT = 0.8 - 0.6 * math.exp(-0.3 * 1)
LINE = 2 * SEQ

HALF = KT // 2 * P
RAW_SLOTS = 4
RING = 4

U_QKV0 = 0
U_OUT0 = U_QKV0 + 3 * A_HEADS + GROUPS
U_FF0 = U_OUT0 + KT
U_QKV1 = U_FF0 + 2 * KT * FF_CHUNKS
U_OUT1 = U_QKV1 + 6 * C_HEADS
U_FF1 = U_OUT1 + KT
UNITS = U_FF1 + 2 * KT * FF_CHUNKS

MID_ATT0, MID_FF0 = 0, KT
MID_ATT1 = MID_FF0 + KT * FF_CHUNKS
MID_FF1 = MID_ATT1 + KT

COPIES_QKV0, COPIES_FF0 = 0, U_OUT0
COPIES_QKV1 = COPIES_FF0 + KT * FF_CHUNKS
COPIES_FF1 = COPIES_QKV1 + 6 * C_HEADS

N_MIX0, N_FFN0, N_MIX1, N_FFN1, N_FINAL = range(5)


def trunk(nc, xT, weights, gains, subln, lambdas, table, w_fnet, onehot, a_head_row, channel_dft,
          position_dft, identity, outT):
    ctx = ExitStack()
    with ctx:
        def sb(name, shape, dt=F32):
            return ctx.enter_context(nc.sbuf_tensor(name, shape, dt))

        def pb(name, shape):
            return ctx.enter_context(nc.psum_tensor(name, shape, F32))

        def sem(name):
            return ctx.enter_context(nc.semaphore(name))

        x = sb("x", [P, KT, SEQ])
        gx = sb("gx", [P, KT, 2 * SEQ], F32R)
        mid = sb("mid", [P, KT, 2 * SEQ], F32R)
        raw = sb("raw", [P, RAW_SLOTS, 2 * HALF])
        w_hi = sb("w_hi", [P, RING, HALF], F32R)
        w_lo = sb("w_lo", [P, RING, HALF], F32R)
        bias = sb("bias", [P, A_HEADS, QT, SEQ])
        y_out = bias[:].rearrange("p h t k -> p (h t k)")[:, 0:KT * SEQ].rearrange(
            "p (f t) -> p f t", f=KT)
        line = bias[0:HEADS, 0, :, :].rearrange("h t k -> h (t k)")
        one_hot = bias[0:BUCKETS + 1, 1, :, :].rearrange("b t k -> b (t k)")
        gain = sb("gain", [P, 5, KT])
        sub_gain = sb("sub_gain", [P, 2])
        sub_gain_in = sb("sub_gain_in", [P, 2])
        lam_in = sb("lam_in", [P, 4])
        lam_prod = sb("lam_prod", [P, 2])
        lam_exp = sb("lam_exp", [P, 2])
        lam_diff = sb("lam_diff", [P, 1])
        neg_lam = sb("neg_lam", [P, 1])
        tab = sb("tab", [BUCKETS + 1, HEADS])
        wf = sb("wf", [P, GROUPS, P])
        ch_dft = sb("ch_dft", [P, 2, P])
        pos_dft = sb("pos_dft", [P, QT, 2, SEQ])
        ch_map = sb("ch_map", [P, GROUPS, 2, P])
        mixed = sb("mixed", [P, QT, 2 * P])
        ident = sb("ident", [P, P])
        ones = sb("ones", [P, P])
        minus_half = sb("minus_half", [P, 2])
        copied = sb("copied", [P, SEQ])
        summed = sb("summed", [P, SEQ])
        relu = sb("relu", [P, SEQ])
        square = sb("square", [P, SEQ])
        x_sq = sb("x_sq", [P, SEQ])
        sum_sq = sb("sum_sq", [P, SEQ])
        rstd = sb("rstd", [P, SEQ])
        mean_sq = sb("mean_sq", [P, QT])
        rstd_col = sb("rstd_col", [P, QT])
        diag = sb("diag", [P, QT, P])
        q_t = sb("q_t", [P, 2, SEQ])
        u_t = q_t[:, 1, :]
        k_t = sb("k_t", [P, 2, SEQ])
        v_t = sb("v_t", [P, 2, SEQ])
        v_tok = sb("v_tok", [P, QT, 2 * P])
        logits = sb("logits", [P, 2, QT, SEQ])
        probs = logits
        row_max = sb("row_max", [P, 2, QT])
        neg_max = sb("neg_max", [P, 2, QT])
        row_sum = sb("row_sum", [P, 2, QT])
        row_inv = sb("row_inv", [P, 2, QT])
        lam_inv = sb("lam_inv", [P, QT])
        part0, o_norm = pos_dft[:, 0, :, :], pos_dft[:, 1, :, :]
        attn = sb("attn", [P, QT, SEQ])
        attn_t = sb("attn_t", [P, QT, SEQ])
        o_sq = mixed
        o_sum = sb("o_sum", [P, QT])
        o_mean = sb("o_mean", [P, QT])
        o_inv = sb("o_inv", [P, QT])

        acc = [pb(f"acc{i}", [P, 2 * SEQ]) for i in range(2)]
        ps_scores = [pb(f"ps_scores{i}", [P, QT, SEQ]) for i in range(2)]
        ps_attn_t = pb("ps_attn_t", [P, QT, SEQ])
        ps_v = pb("ps_v", [P, QT, 2 * P])
        ps_o = pb("ps_o", [P, 2 * SEQ])
        ps_aux = pb("ps_aux", [P, 2 * SEQ])

        bias_line = nc.dram_tensor("bias_line", (HEADS, LINE), F32, kind="Internal").ap()

        raw_landed = [sem(f"raw_landed{i}") for i in range(RAW_SLOTS)]
        hi_ready, lo_ready = sem("hi_ready"), sem("lo_ready")
        w_used = sem("w_used")
        acc_free = sem("acc_free")
        acc_half = sem("acc_half")
        copy_ready = sem("copy_ready")
        proj_ready = sem("proj_ready")
        relu_done, squared = sem("relu_done"), sem("squared")
        mid_hi, mid_ready = sem("mid_hi"), sem("mid_ready")
        gx_hi, gx_ready = sem("gx_hi"), sem("gx_ready")
        xsq_done, sum_steps = sem("xsq_done"), sem("sum_steps")
        stat_ready, mean_ready = sem("stat_ready"), sem("mean_ready")
        inv_ready, diag_ready = sem("inv_ready"), sem("diag_ready")
        bcast_ready, rstd_ready = sem("bcast_ready"), sem("rstd_ready")
        scores_ready, scores_read = sem("scores_ready"), sem("scores_read")
        max_done, neg_ready, exp_done = sem("max_done"), sem("neg_ready"), sem("exp_done")
        soft_steps, attn_ready = sem("soft_steps"), sem("attn_ready")
        vt_ready, pt_ready = sem("vt_ready"), sem("pt_ready")
        v_copied, pt_copied, o_ready = sem("v_copied"), sem("pt_copied"), sem("o_ready")
        osq_done, omean_ready = sem("osq_done"), sem("omean_ready")
        oinv_ready, onorm_ready, ot_ready = sem("oinv_ready"), sem("onorm_ready"), sem("ot_ready")
        mix1_ready, mix_copied, mix2_ready = sem("mix1_ready"), sem("mix_copied"), sem("mix2_ready")
        x_landed = [sem(f"x_landed{i}") for i in range(4)]
        small_landed, tab_landed, dft_landed = sem("small_landed"), sem("tab_landed"), sem("dft_landed")
        gain_landed, ones_ready = sem("gain_landed"), sem("ones_ready")
        map_ready, map_copied = sem("map_ready"), sem("map_copied")
        line_ready, line_copied, line_stored = sem("line_ready"), sem("line_copied"), sem("line_stored")
        bias_landed = [sem(f"bias_landed{i}") for i in range(2)]
        lam_steps, lam_sum_ready, lam_exp_ready = sem("lam_steps"), sem("lam_sum_ready"), sem("lam_exp_ready")
        y_ready, y_stored = sem("y_ready"), sem("y_stored")

        block = ctx.enter_context(nc.Block())

        @block.sync
        def _(sp):
            def load(u, o=0, free=True):
                slot = u % RAW_SLOTS
                if free:
                    sp.wait_ge(lo_ready, 2 * (u - RAW_SLOTS + 1) + 2 * o)
                sp.dma_start(raw[:, slot, :], weights[u + o]).then_inc(raw_landed[slot], 16)

            for u in range(RAW_SLOTS):
                load(u, free=False)
            with sp.Fori(0, UNITS // RAW_SLOTS - 1) as i:
                for s in range(RAW_SLOTS):
                    load(RAW_SLOTS + s, RAW_SLOTS * i)
            for g in range(4):
                sp.wait_ge(y_ready, g + 1)
                sp.dma_start(outT.rearrange("(f p) t -> p f t", p=P)[:, 4 * g:4 * g + 4, :],
                             y_out[:, 4 * g:4 * g + 4, :]).then_inc(y_stored, 16)
            sp.wait_ge(y_stored, 16 * 4)

        @block.gpsimd
        def _(pool):
            pool.memset(ones[:], 1.0)
            pool.memset(minus_half[:], -0.5).then_inc(ones_ready, 1)
            pool.wait_ge(ones_ready, 1)

            def token_inverse(n):
                pool.wait_ge(mean_ready, n + 1)
                pool.tensor_tensor(rstd_col[:], mean_sq[:], minus_half[:], ALU.pow).then_inc(inv_ready, 1)

            token_inverse(N_MIX0)
            token_inverse(N_FFN0)
            token_inverse(N_MIX1)
            with pool.Fori(0, C_HEADS) as h:
                pool.wait_ge(omean_ready, h + 1)
                pool.tensor_tensor(o_inv[:], o_mean[:], minus_half[:], ALU.pow).then_inc(oinv_ready, 1)
            token_inverse(N_FFN1)
            token_inverse(N_FINAL)

        @block.scalar
        def _(act):
            def split_hi(n, o=0):
                u, part = n // 2, n % 2
                if part == 0:
                    act.wait_ge(raw_landed[u % RAW_SLOTS], 16 * (u // RAW_SLOTS + 1) + 16 // RAW_SLOTS * o)
                if n >= RING:
                    act.wait_ge(w_used, n - RING + 1 + 2 * o)
                act.activation(w_hi[:, n % RING, :], raw[:, u % RAW_SLOTS, part * HALF:(part + 1) * HALF],
                               ACT.Copy).then_inc(hi_ready, 1)

            def copy_cross(u, o):
                act.wait_ge(w_used, 2 * u + 2 + 2 * o)
                act.wait_ge(acc_free, u + o)
                act.activation(copied[:], acc[u % 2][:, SEQ:], ACT.Copy).then_inc(copy_ready, 1)

            def unit(u, o=0, before=(), first=(), second=(), copy=True, split=True):
                for step in before:
                    step()
                if split:
                    split_hi(2 * u + 4, o)
                for step in first:
                    step()
                if copy:
                    copy_cross(u, o)
                if split:
                    split_hi(2 * u + 5, o)
                for step in second:
                    step()

            def gx_part(n, f, of=0):
                t = f + of
                act.wait_ge(sum_steps, 17 * n + 1 + t)
                dst = y_out[:, t, :] if n == N_FINAL else gx[:, t, 0:SEQ]
                act.activation(dst, x[:, t, :], ACT.Copy, scale=gain[:, n, bass.ts(t, 1)]).then_inc(gx_hi, 1)
                act.activation(x_sq[:], x[:, t, :], ACT.Square).then_inc(xsq_done, 1)

            def residual(n, u, f, o=0, of=0):
                def step():
                    act.wait_ge(acc_free, u + 1 + o)
                    gx_part(n, f, of)
                return step

            def exps(m, s, head, heads_before, os=0, oh=0):
                def step():
                    act.wait_ge(neg_ready, s + 1 + os)
                    act.wait_ge(attn_ready, QT * (heads_before + oh))
                    for t in range(QT):
                        act.activation(probs[:, m, t, :], logits[:, m, t, :], ACT.Exp,
                                       bias=neg_max[:, m, t:t + 1],
                                       accum_out=row_sum[:, m, t:t + 1]).then_inc(exp_done, 1)
                return step

            def copy_v(n, width, oh=0):
                def step():
                    act.wait_ge(vt_ready, n + 1 + oh)
                    act.wait_ge(o_ready, n + oh)
                    act.activation(v_tok[:, :, 0:width], ps_v[:, :, 0:width], ACT.Copy).then_inc(v_copied, 1)
                return step

            def copy_attn(n, oh=0):
                def step():
                    act.wait_ge(pt_ready, n + 1 + oh)
                    act.wait_ge(o_ready, n + oh)
                    act.activation(attn_t[:], ps_attn_t[:, :, ::-1], ACT.Copy).then_inc(pt_copied, 1)
                return step

            def load_bias(layer):
                first, n = ((0, A_HEADS), (A_HEADS, C_HEADS))[layer]
                for t in range(QT):
                    src = bass.AP(bias_line.tensor, first * LINE + P * t, [[1, P], [LINE, n], [1, SEQ]])
                    act.dma_start(bias[:, 0:n, t, :], src).then_inc(bias_landed[layer], 16)

            for g in range(4):
                act.dma_start(x[:, 4 * g:4 * g + 4, :], xT.rearrange("(f p) t -> p f t", p=P)[:, 4 * g:4 * g + 4, :]
                              ).then_inc(x_landed[g], 16)
                if g == 0:
                    act.dma_start(gain[:], gains).then_inc(gain_landed, 16)
            act.dma_start(tab[0:BUCKETS, :], table).then_inc(tab_landed, 16)
            act.dma_start(tab[BUCKETS:BUCKETS + 1, :], a_head_row).then_inc(tab_landed, 16)
            act.dma_start(one_hot, onehot).then_inc(tab_landed, 16)
            act.dma_start(ident[:], identity).then_inc(small_landed, 16)
            act.dma_start(lam_in[:], lambdas).then_inc(small_landed, 16)
            act.dma_start(sub_gain_in[:], subln).then_inc(small_landed, 16)
            act.dma_start(wf[:], w_fnet.rearrange("g c e -> c g e")).then_inc(dft_landed, 16)
            act.dma_start(ch_dft[:], channel_dft).then_inc(dft_landed, 16)
            act.dma_start(pos_dft[:], position_dft).then_inc(dft_landed, 16)

            act.wait_ge(gain_landed, 16)
            for f in range(KT):
                act.wait_ge(x_landed[f // 4], 16)
                gx_part(N_MIX0, f)
                if f % 4 == 0:
                    split_hi(f // 4)
            act.wait_ge(line_ready, 1)
            act.activation(line, ps_scores[0][0:HEADS, :, :].rearrange("h t k -> h (t k)"), ACT.Copy).then_inc(line_copied, 1)
            act.wait_ge(line_copied, 1)
            act.dma_start(bias_line, line).then_inc(line_stored, 16)
            act.wait_ge(line_stored, 16)
            load_bias(0)
            act.wait_ge(map_ready, 1)
            act.activation(ch_map[:, :, 0, :], ps_o[:].rearrange("p (g e) -> p g e", g=GROUPS), ACT.Copy)
            act.activation(ch_map[:, :, 1, :], ps_attn_t[:].rearrange("p t (g e) -> p (t g) e", e=P), ACT.Copy
                           ).then_inc(map_copied, 1)
            act.wait_ge(lam_sum_ready, 1)
            act.activation(lam_exp[:], ps_v[:, 0, 0:2], ACT.Exp).then_inc(lam_exp_ready, 1)

            unit(0)
            unit(1)

            def hi_att0(h, oh):
                def step():
                    act.wait_ge(o_ready, h + 1 + oh)
                    act.activation(mid[:, h + oh, 0:SEQ], ps_o[:, 0:SEQ], ACT.Copy).then_inc(mid_hi, 1)
                return step

            def copy_mixed(g):
                def step():
                    act.wait_ge(mix1_ready, g + 1)
                    act.wait_ge(mix2_ready, g)
                    act.activation(mixed[:], ps_scores[1][:], ACT.Copy).then_inc(mix_copied, 1)
                return step

            def hi_mix(g):
                def step():
                    act.wait_ge(mix2_ready, g + 1)
                    act.activation(mid[:, A_HEADS + g, 0:SEQ], ps_aux[:, 0:SEQ], ACT.Copy).then_inc(mid_hi, 1)
                return step

            def head0(h, oh=0):
                u, o = 2 + 3 * h, 3 * oh
                unit(u, o, first=[exps(0, h, h, h, oh, oh)])
                unit(u + 1, o, first=[copy_v(h, P, oh), copy_attn(h, oh)])
                if h < A_HEADS - 1:
                    unit(u + 2, o, first=[hi_att0(h, oh)])
                else:
                    unit(u + 2, o, first=[hi_att0(h, oh), copy_mixed(0)], second=[hi_mix(0)])

            with act.Fori(0, 2) as i:
                for h in range(4):
                    head0(h, 4 * i)
            for h in range(8, A_HEADS):
                head0(h)
            for g in (1, 2):
                unit(U_OUT0 - 3 + g, first=[copy_mixed(g)], second=[hi_mix(g)])

            def out_projection(u0, n, before=(), first=(), second=()):
                for step in before:
                    step()
                split_hi(2 * u0 + 4)
                for step in first:
                    step()
                split_hi(2 * u0 + 5)
                for step in second:
                    step()
                split_hi(2 * u0 + 6)
                residual(n, u0, 0)()
                split_hi(2 * u0 + 7)
                residual(n, u0 + 1, 1)()
                for f in (2, 3):
                    unit(u0 + f, copy=False, second=[residual(n, u0 + f, f)])
                with act.Fori(1, 4) as i:
                    for s in range(4):
                        unit(u0 + s, 4 * i, copy=False, second=[residual(n, u0 + s, s, 4 * i, 4 * i)])

            out_projection(U_OUT0, N_FFN0, first=[copy_mixed(3)], second=[hi_mix(3)])
            load_bias(1)

            def hidden(u, f, k, o=0, of=0, ok=0, chunk=0):
                def hi_hidden():
                    act.wait_ge(squared, k + 1 + ok)
                    act.activation(mid[:, f + of, 0:SEQ], square[:], ACT.Copy).then_inc(mid_hi, 1)
                unit(u, o, second=[hi_hidden])

            def output(u, f, k, o=0, of=0, ok=0, chunk=0):
                unit(u, o, copy=False)

            def last_output(n):
                def run(u, f, k, o=0, of=0, ok=0, chunk=0):
                    unit(u, o, copy=False, second=[residual(n, u, f, o, of)], split=u + 2 < UNITS)
                return run

            feed_forward(act, 0, U_FF0, hidden, output, last_output(N_MIX1))

            unit(U_QKV1)
            unit(U_QKV1 + 1)

            def squares(h, oh=0):
                def step():
                    act.wait_ge(o_ready, A_HEADS + h + 1 + oh)
                    act.wait_ge(osq_done, QT * (h + oh))
                    for t in range(QT):
                        act.activation(o_sq[:, t, :], ps_o[:, t * SEQ:(t + 1) * SEQ], ACT.Square,
                                       accum_out=o_sum[:, t:t + 1]).then_inc(osq_done, 1)
                return step

            def hi_att1(h, oh=0):
                def step():
                    act.wait_ge(ot_ready, h + 1 + oh)
                    for j in range(2):
                        act.activation(mid[:, 2 * h + j + 2 * oh, 0:SEQ], ps_aux[:, j * SEQ:(j + 1) * SEQ], ACT.Copy,
                                       scale=sub_gain[:, j:j + 1]).then_inc(mid_hi, 1)
                return step

            def head1(h, oh=0):
                u, o, g = U_QKV1 + 2 + 6 * h, 6 * oh, A_HEADS + h
                unit(u, o, first=[exps(0, A_HEADS + 2 * h, h, g, 2 * oh, oh)])
                unit(u + 1, o)
                unit(u + 2, o, first=[exps(1, A_HEADS + 2 * h + 1, h, g, 2 * oh, oh)])
                unit(u + 3, o, first=[copy_attn(g, oh)])
                if h < C_HEADS - 1:
                    unit(u + 4, o, first=[copy_v(g, 2 * P, oh)])
                    unit(u + 5, o, before=[squares(h, oh)], second=[hi_att1(h, oh)])

            with act.Fori(0, 3) as i:
                for h in range(2):
                    head1(h, 2 * i)
            head1(6)
            head1(7)
            out_projection(U_OUT1, N_FFN1, before=[copy_v(HEADS - 1, 2 * P)], first=[squares(C_HEADS - 1)],
                           second=[hi_att1(C_HEADS - 1)])
            feed_forward(act, 1, U_FF1, hidden, output, last_output(N_FINAL))

        @block.vector
        def _(dve):
            def split_lo(n, o=0):
                u, part = n // 2, n % 2
                dve.wait_ge(hi_ready, n + 1 + 2 * o)
                dve.tensor_tensor(w_lo[:, n % RING, :], raw[:, u % RAW_SLOTS, part * HALF:(part + 1) * HALF],
                                  w_hi[:, n % RING, :].bitcast(F32), ALU.subtract).then_inc(lo_ready, 1)

            def sum_product(u, c, o=0, oc=0):
                dve.wait_ge(copy_ready, c + 1 + oc)
                dve.tensor_tensor(summed[:], acc[u % 2][:, 0:SEQ], copied[:], ALU.add).then_inc(acc_free, 1)
                dve.wait_ge(acc_free, u + 1 + o)

            def projected(u, c, dst, scale=1.0, o=0, oc=0):
                def step():
                    p = c if u < U_OUT0 else c - FF_CHUNKS * KT
                    dve.wait_ge(proj_ready, p + oc)
                    sum_product(u, c, o, oc)
                    dve.scalar_tensor_tensor(dst, summed[:], scale, rstd[:], ALU.mult, ALU.mult
                                             ).then_inc(proj_ready, 1)
                return step

            def add_to_residual(u, f, r, o=0, of=0, r_o=0, late=0):
                def step():
                    t = f + of
                    dve.wait_ge(w_used, 2 * u + 2 + late + 2 * o)
                    dve.tensor_tensor(x[:, t, :], x[:, t, :], acc[u % 2][:, 0:SEQ], ALU.add).then_inc(acc_half, 1)
                    dve.wait_ge(acc_half, r + 1 + r_o)
                    dve.tensor_tensor(x[:, t, :], x[:, t, :], acc[u % 2][:, SEQ:], ALU.add).then_inc(acc_free, 1)
                return step

            def gx_rest(n, f, of=0):
                def step():
                    t = f + of
                    dve.wait_ge(gx_hi, KT * n + t + 1)
                    if n != N_FINAL:
                        dve.scalar_tensor_tensor(gx[:, t, SEQ:], x[:, t, :], gain[:, n, bass.ts(t, 1)],
                                                 gx[:, t, 0:SEQ].bitcast(F32), ALU.mult, ALU.subtract
                                                 ).then_inc(gx_ready, 1)
                    dve.wait_ge(xsq_done, KT * n + t + 1)
                    dve.wait_ge(sum_steps, 17 * n + 1 + t)
                    dve.tensor_tensor(sum_sq[:], sum_sq[:], x_sq[:], ALU.add).then_inc(sum_steps, 1)
                return step

            def clear_sum():
                dve.memset(sum_sq[:], 0.0).then_inc(sum_steps, 1)

            def unit(u, evac, o=0, before=(), first=(), mid_steps=(), second=(), split=True):
                for step in before:
                    step()
                if split:
                    split_lo(2 * u + 4, o)
                for step in first:
                    step()
                evac()
                if split:
                    split_lo(2 * u + 5, o)
                for step in second:
                    step()

            def token_stats(n):
                dve.wait_ge(stat_ready, n + 1)
                dve.tensor_scalar(mean_sq[:], ps_aux[:, 0:QT], 1.0 / D, EPS, ALU.mult, ALU.add
                                  ).then_inc(mean_ready, 1)
                dve.wait_ge(inv_ready, n + 1)
                for t in range(QT):
                    dve.tensor_scalar(diag[:, t, :], ident[:], rstd_col[:, t:t + 1], None, ALU.mult
                                      ).then_inc(diag_ready, 1)

            def token_rstd(n):
                dve.wait_ge(bcast_ready, n + 1)
                dve.tensor_copy(rstd[:], ps_aux[:, 0:SEQ]).then_inc(rstd_ready, 1)
                dve.wait_ge(rstd_ready, n + 1)

            def first_unit(u, n, evac, second=()):
                split_lo(2 * u + 4)
                token_stats(n)
                split_lo(2 * u + 5)
                token_rstd(n)
                evac()
                for step in second:
                    step()

            def score_rows(m, s, before, head, os=0, ob=0, oh=0):
                def step():
                    dve.wait_ge(scores_ready, s + 1 + os)
                    dve.wait_ge(exp_done, before + ob)
                    dve.tensor_tensor(logits[:, m, :, :], ps_scores[m][:], bias[:, head + oh, :, :], ALU.add
                                      ).then_inc(scores_read, 1)
                    dve.wait_ge(scores_read, s + 1 + os)
                    dve.tensor_reduce(row_max[:, m, :], logits[:, m, :, :], AX_X, ALU.max).then_inc(max_done, 1)
                    dve.wait_ge(max_done, s + 1 + os)
                    dve.tensor_scalar(neg_max[:, m, :], row_max[:, m, :], -1.0, None, ALU.mult
                                      ).then_inc(neg_ready, 1)
                return step

            clear_sum()
            dve.wait_ge(gain_landed, 16)
            for f in range(KT):
                dve.wait_ge(x_landed[f // 4], 16)
                gx_rest(N_MIX0, f)()
                if f % 4 == 0:
                    split_lo(f // 4)
            dve.wait_ge(small_landed, 16 * 3)
            dve.tensor_tensor(lam_prod[:], lam_in[:, 0:4:2], lam_in[:, 1:4:2], ALU.mult).then_inc(lam_steps, 1)
            dve.tensor_scalar(sub_gain[:], sub_gain_in[:], 1.0 - LAMBDA_INIT, None, ALU.mult).then_inc(lam_steps, 1)
            dve.wait_ge(lam_exp_ready, 1)
            dve.tensor_tensor(lam_diff[:], lam_exp[:, 1:2], lam_exp[:, 0:1], ALU.subtract).then_inc(lam_steps, 1)
            dve.wait_ge(lam_steps, 3)
            dve.tensor_scalar(neg_lam[:], lam_diff[:], -LAMBDA_INIT, None, ALU.add).then_inc(lam_steps, 1)

            q0, k0, v0 = q_t[:, 0, ::-1], k_t[:, 0, :], v_t[:, 0, :]
            first_unit(0, N_MIX0, projected(0, 0, q0, SCALE))
            unit(1, projected(1, 1, k0))
            dve.wait_ge(bias_landed[0], 16 * QT)

            def normalise(h, oh=0):
                def step():
                    dve.wait_ge(exp_done, QT * (h + 1) + QT * oh)
                    dve.wait_ge(attn_ready, QT * (h + oh))
                    dve.reciprocal(row_inv[:, 0, :], row_sum[:, 0, :]).then_inc(soft_steps, 1)
                    dve.wait_ge(soft_steps, h + 1 + oh)
                    dve.wait_ge(pt_ready, h + oh)
                    for t in range(QT):
                        dve.tensor_scalar(attn[:, t, :], probs[:, 0, t, :], row_inv[:, 0, t:t + 1], None, ALU.mult
                                          ).then_inc(attn_ready, 1)
                return step

            def lo_part(tile, src, ot=0):
                def step():
                    dve.wait_ge(mid_hi, tile + 1 + ot)
                    dve.tensor_tensor(mid[:, tile + ot, SEQ:], src, mid[:, tile + ot, 0:SEQ].bitcast(F32),
                                      ALU.subtract).then_inc(mid_ready, 1)
                return step

            def head0(h, oh=0):
                u, o = 2 + 3 * h, 3 * oh
                last = h == A_HEADS - 1
                unit(u, projected(u, u, v0, 1.0, o, o), o,
                     first=[score_rows(0, h, QT * h, h, oh, QT * oh, oh), normalise(h, oh)])
                unit(u + 1, projected(u + 1, u + 1, u_t if last else q0, 1.0 if last else SCALE, o, o), o)
                unit(u + 2, projected(u + 2, u + 2, u_t if last else k0, 1.0, o, o), o,
                     first=[lo_part(h, ps_o[:, 0:SEQ], oh)],
                     second=[lo_part(A_HEADS, ps_aux[:, 0:SEQ])] if last else [])

            with dve.Fori(0, 2) as i:
                for h in range(4):
                    head0(h, 4 * i)
            for h in range(8, A_HEADS):
                head0(h)
            for g in (1, 2):
                u = U_OUT0 - 3 + g
                unit(u, projected(u, u, u_t), second=[lo_part(A_HEADS + g, ps_aux[:, 0:SEQ])])

            def out_projection(u0, n, r, first=(), second=()):
                clear_sum()
                split_lo(2 * u0 + 4)
                for step in first:
                    step()
                split_lo(2 * u0 + 5)
                for step in second:
                    step()
                add_to_residual(u0, 0, r, late=1)()
                split_lo(2 * u0 + 6)
                gx_rest(n, 0)()
                add_to_residual(u0 + 1, 1, r + 1)()
                split_lo(2 * u0 + 7)
                gx_rest(n, 1)()
                for f in (2, 3):
                    unit(u0 + f, add_to_residual(u0 + f, f, r + f), second=[gx_rest(n, f)])
                with dve.Fori(1, 4) as i:
                    for s in range(4):
                        unit(u0 + s, add_to_residual(u0 + s, s, r + s, 4 * i, 4 * i, 4 * i), 4 * i,
                             second=[gx_rest(n, s, 4 * i)])

            out_projection(U_OUT0, N_FFN0, 0, second=[lo_part(KT - 1, ps_aux[:, 0:SEQ])])

            def hidden_in(layer):
                c0 = (COPIES_FF0, COPIES_FF1)[layer]
                m0 = (MID_FF0, MID_FF1)[layer]
                k0 = layer * FF_CHUNKS * KT

                def run(u, f, k, o=0, of=0, ok=0, chunk=0):
                    c, k_in = c0 + k - k0, k

                    def evac():
                        sum_product(u, c, o, ok)
                        dve.scalar_tensor_tensor(relu[:], summed[:], 0.0, rstd[:], ALU.max, ALU.mult
                                                 ).then_inc(relu_done, 1)
                        dve.wait_ge(relu_done, k_in + 1 + ok)
                        dve.wait_ge(mid_ready, m0 + k - k0 + ok)
                        dve.tensor_tensor(square[:], relu[:], relu[:], ALU.mult).then_inc(squared, 1)

                    def lo_hidden():
                        dve.wait_ge(mid_hi, m0 + k - k0 + 1 + ok)
                        dve.tensor_tensor(mid[:, f + of, SEQ:], square[:], mid[:, f + of, 0:SEQ].bitcast(F32),
                                          ALU.subtract).then_inc(mid_ready, 1)

                    if f == 0 and isinstance(o, int) and u in (U_FF0, U_FF1):
                        first_unit(u, (N_FFN0, N_FFN1)[layer], evac, second=[lo_hidden])
                    else:
                        unit(u, evac, o, second=[lo_hidden])
                return run

            def output_in(r0, layer):
                def run(u, f, k, o=0, of=0, ok=0, chunk=0):
                    r = r0 + k - layer * FF_CHUNKS * KT
                    unit(u, add_to_residual(u, f, r, o, of, ok), o)
                return run

            def last_output_in(r0, layer, n):
                def run(u, f, k, o=0, of=0, ok=0, chunk=0):
                    r = r0 + k - layer * FF_CHUNKS * KT
                    unit(u, add_to_residual(u, f, r, o, of, ok), o, second=[gx_rest(n, f, of)],
                         split=u + 2 < UNITS)
                return run

            dve.wait_ge(proj_ready, U_OUT0)
            feed_forward(dve, 0, U_FF0, hidden_in(0), output_in(KT, 0), last_output_in(KT, 0, N_MIX1),
                         clear_sum)

            first_unit(U_QKV1, N_MIX1, projected(U_QKV1, COPIES_QKV1, q0, SCALE))
            unit(U_QKV1 + 1, projected(U_QKV1 + 1, COPIES_QKV1 + 1, k0))
            dve.wait_ge(bias_landed[1], 16 * QT)
            dve.wait_ge(lam_steps, 4)

            def combine(h, oh=0):
                def step():
                    n = A_HEADS + 4 * h
                    dve.wait_ge(exp_done, QT * A_HEADS + 4 * (h + 1) + 4 * oh)
                    dve.wait_ge(attn_ready, QT * (A_HEADS + h + oh))
                    dve.reciprocal(row_inv[:], row_sum[:]).then_inc(soft_steps, 1)
                    dve.wait_ge(soft_steps, n + 1 + 4 * oh)
                    dve.tensor_scalar(lam_inv[:], row_inv[:, 1, :], neg_lam[:], None, ALU.mult
                                      ).then_inc(soft_steps, 1)
                    for t in range(QT):
                        dve.tensor_scalar(part0[:, t, :], probs[:, 0, t, :], row_inv[:, 0, t:t + 1], None, ALU.mult
                                          ).then_inc(soft_steps, 1)
                    dve.wait_ge(soft_steps, n + 4 + 4 * oh)
                    dve.wait_ge(pt_ready, A_HEADS + h + oh)
                    for t in range(QT):
                        dve.scalar_tensor_tensor(attn[:, t, :], probs[:, 1, t, :], lam_inv[:, t:t + 1],
                                                 part0[:, t, :], ALU.mult, ALU.add).then_inc(attn_ready, 1)
                return step

            def head_norm(h, oh=0):
                def step():
                    dve.wait_ge(osq_done, QT * (h + 1 + oh))
                    dve.tensor_scalar(o_mean[:], o_sum[:], 1.0 / (2 * P), EPS, ALU.mult, ALU.add
                                      ).then_inc(omean_ready, 1)
                    dve.wait_ge(oinv_ready, h + 1 + oh)
                    dve.wait_ge(ot_ready, h + oh)
                    for t in range(QT):
                        dve.tensor_scalar(o_norm[:, t, :], ps_o[:, t * SEQ:(t + 1) * SEQ], o_inv[:, t:t + 1], None,
                                          ALU.mult).then_inc(onorm_ready, 1)
                return step

            def lo_att1(h, oh=0):
                def step():
                    dve.wait_ge(mid_hi, MID_ATT1 + 2 * (h + 1) + 2 * oh)
                    for j in range(2):
                        t = 2 * h + j + 2 * oh
                        dve.scalar_tensor_tensor(mid[:, t, SEQ:], ps_aux[:, j * SEQ:(j + 1) * SEQ],
                                                 sub_gain[:, j:j + 1], mid[:, t, 0:SEQ].bitcast(F32),
                                                 ALU.mult, ALU.subtract).then_inc(mid_ready, 1)
                return step

            def head1(h, oh=0):
                u, c = U_QKV1 + 2 + 6 * h, COPIES_QKV1 + 2 + 6 * h
                o, s, e = 6 * oh, A_HEADS + 2 * h, QT * A_HEADS + 4 * h

                def proj(k, dst, scale=1.0):
                    return projected(u + k, c + k, dst, scale, o, o)

                unit(u, proj(0, q_t[:, 1, ::-1], SCALE), o, first=[score_rows(0, s, e, h, 2 * oh, 4 * oh, oh)])
                unit(u + 1, proj(1, k_t[:, 1, :]), o)
                unit(u + 2, proj(2, v_t[:, 0, :]), o,
                     first=[score_rows(1, s + 1, e, h, 2 * oh, 4 * oh, oh), combine(h, oh)])
                unit(u + 3, proj(3, v_t[:, 1, :]), o)
                if h < C_HEADS - 1:
                    unit(u + 4, proj(4, q0, SCALE), o)
                    unit(u + 5, proj(5, k0), o, before=[head_norm(h, oh)], second=[lo_att1(h, oh)])

            with dve.Fori(0, 3) as i:
                for h in range(2):
                    head1(h, 2 * i)
            head1(6)
            head1(7)
            out_projection(U_OUT1, N_FFN1, KT * (1 + FF_CHUNKS), first=[head_norm(C_HEADS - 1)],
                           second=[lo_att1(C_HEADS - 1)])
            dve.wait_ge(proj_ready, U_OUT0 + 6 * C_HEADS)
            feed_forward(dve, 1, U_FF1, hidden_in(1), output_in(KT * (2 + FF_CHUNKS), 1),
                         last_output_in(KT * (2 + FF_CHUNKS), 1, N_FINAL), clear_sum)

            token_stats(N_FINAL)
            token_rstd(N_FINAL)
            for g in range(4):
                for f in range(4 * g, 4 * g + 4):
                    ins = dve.tensor_tensor(y_out[:, f, :], y_out[:, f, :], rstd[:], ALU.mult)
                ins.then_inc(y_ready, 1)

        @block.tensor
        def _(pe):
            def half(n, bank, kts, operand, o=0, hooks=None, whole=None, tile_wait=None):
                hooks = hooks or {}
                pe.wait_ge(lo_ready, n + 1 + 2 * o)
                for j, kt in enumerate(kts):
                    for step in hooks.get(j, ()):
                        step()
                    if tile_wait is not None and (kt >= KT // 2 or kt == 0):
                        ready, base = tile_wait
                        pe.wait_ge(ready, base + (kt + 1 if kt else KT // 2))
                    cols = slice(j * P, (j + 1) * P)

                    def hi():
                        return pe.matmul(acc[bank][:], w_hi[:, n % RING, cols], operand[:, kt, :], start=kt == 0,
                                         stop=kt == KT - 1)

                    def lo():
                        return pe.matmul(acc[bank][:, SEQ:], w_lo[:, n % RING, cols], operand[:, kt, 0:SEQ],
                                         start=False, stop=False)

                    if kt == KT - 1:
                        lo()
                        ins = hi()
                    else:
                        hi()
                        ins = lo()
                ins.then_inc(w_used, 1)
                for step in hooks.get(KT // 2, ()):
                    step()

            FIRST, SECOND = range(0, KT // 2), range(KT // 2, KT)

            def unit(u, operand, o=0, hooks=({}, {}), tile_wait=None):
                if u >= 2:
                    pe.wait_ge(acc_free, u - 1 + o)
                half(2 * u, u % 2, FIRST, operand, o, hooks[0], tile_wait=tile_wait)
                half(2 * u + 1, u % 2, SECOND, operand, o, hooks[1], tile_wait=tile_wait)

            def stat_sum(n):
                def step():
                    pe.wait_ge(sum_steps, 17 * (n + 1))
                    for t in range(QT):
                        ins = pe.matmul(ps_aux[:, t:t + 1], sum_sq[:, t * P:(t + 1) * P], ones[:, 0:1],
                                        start=True, stop=True)
                    ins.then_inc(stat_ready, 1)
                return step

            def stat_spread(n):
                def step():
                    pe.wait_ge(diag_ready, QT * (n + 1))
                    for t in range(QT):
                        ins = pe.matmul(ps_aux[:, t * P:(t + 1) * P], ones[:], diag[:, t, :], start=True, stop=True)
                    ins.then_inc(bcast_ready, 1)
                return step

            def scores(m, s, proj, read, os=0, op=0, orr=0):
                def step():
                    pe.wait_ge(proj_ready, proj + op)
                    pe.wait_ge(scores_read, read + orr)
                    for t in range(QT):
                        ins = pe.matmul(ps_scores[m][:, t, :], q_t[:, m, t * P:(t + 1) * P], k_t[:, m, :],
                                        start=True, stop=True)
                    ins.then_inc(scores_ready, 1)
                return step

            def turn_v(n, proj, tiles, oh=0, op=0):
                def step():
                    pe.wait_ge(proj_ready, proj + op)
                    pe.wait_ge(v_copied, n + oh)
                    for kt in range(QT):
                        for j in range(tiles):
                            ins = pe.transpose(ps_v[:, kt, j * P:(j + 1) * P], v_t[:, j, kt * P:(kt + 1) * P], ident[:])
                    ins.then_inc(vt_ready, 1)
                return step

            def turn_attn(n, oh=0):
                def step():
                    pe.wait_ge(attn_ready, QT * (n + 1) + QT * oh)
                    pe.wait_ge(pt_copied, n + oh)
                    for kt in range(QT):
                        for t in range(QT):
                            ins = pe.transpose(ps_attn_t[:, kt, t * P:(t + 1) * P], attn[:, t, kt * P:(kt + 1) * P],
                                               ident[:])
                    ins.then_inc(pt_ready, 1)
                return step

            def attend0(h, oh=0):
                def step():
                    pe.wait_ge(v_copied, h + 1 + oh)
                    pe.wait_ge(pt_copied, h + 1 + oh)
                    pe.wait_ge(mid_ready, h + oh)
                    for kt in range(QT):
                        ins = pe.matmul(ps_o[:, 0:SEQ], v_tok[:, kt, 0:P], attn_t[:, kt, :], start=kt == 0,
                                        stop=kt == QT - 1)
                    ins.then_inc(o_ready, 1)
                return step

            def mix_channels(g):
                def step():
                    pe.wait_ge(proj_ready, 3 * A_HEADS + g + 1)
                    pe.wait_ge(mix_copied, g)
                    for t in range(QT):
                        ins = pe.matmul(ps_scores[1][:, t, :], u_t[:, t * P:(t + 1) * P],
                                        ch_map[:, g, :, :].rearrange("p r e -> p (r e)"), start=True, stop=True)
                    ins.then_inc(mix1_ready, 1)
                return step

            def mix_positions(g):
                def step():
                    pe.wait_ge(mix_copied, g + 1)
                    pe.wait_ge(mid_ready, A_HEADS + g)
                    for t in range(QT):
                        for r in range(2):
                            ins = pe.matmul(ps_aux[:, 0:SEQ], mixed[:, t, r * P:(r + 1) * P], pos_dft[:, t, r, :],
                                            start=t == r == 0, stop=t == r == 1)
                    ins.then_inc(mix2_ready, 1)
                return step

            pe.wait_ge(ones_ready, 1)
            pe.wait_ge(tab_landed, 16 * 3)
            pe.matmul(ps_scores[0][0:HEADS, :, :].rearrange("p t k -> p (t k)"), tab[:], one_hot, start=True,
                      stop=True).then_inc(line_ready, 1)

            def group_maps():
                pe.wait_ge(dft_landed, 16 * 3)
                for r, bank in enumerate((ps_o[:], ps_attn_t[:].rearrange("p t k -> p (t k)"))):
                    for g in range(GROUPS):
                        ins = pe.matmul(bank[:, g * P:(g + 1) * P], ch_dft[:, r, :], wf[:, g, :], start=True, stop=True)
                ins.then_inc(map_ready, 1)
                pe.wait_ge(lam_steps, 1)
                pe.matmul(ps_v[:, 0, 0:2], ones[:], lam_prod[:], start=True, stop=True).then_inc(lam_sum_ready, 1)
                pe.wait_ge(small_landed, 16 * 3)

            unit(0, gx, tile_wait=(gx_ready, 0), hooks=({8: [group_maps]}, {4: [stat_sum(N_MIX0)]}))
            unit(1, gx, hooks=({4: [stat_spread(N_MIX0)]}, {}))
            pe.wait_ge(line_copied, 1)
            pe.wait_ge(map_copied, 1)
            pe.wait_ge(lam_exp_ready, 1)

            def head0(h, oh=0):
                u, o = 2 + 3 * h, 3 * oh
                unit(u, gx, o, hooks=({8: [scores(0, h, u, h, oh, o, oh)]}, {}))
                unit(u + 1, gx, o, hooks=({8: [turn_v(h, u + 1, 1, oh, o), turn_attn(h, oh)]}, {}))
                if h < A_HEADS - 1:
                    unit(u + 2, gx, o, hooks=({8: [attend0(h, oh)]}, {}))
                else:
                    unit(u + 2, gx, o, hooks=({8: [attend0(h, oh), mix_channels(0)]}, {8: [mix_positions(0)]}))

            with pe.Fori(0, 2) as i:
                for h in range(4):
                    head0(h, 4 * i)
            for h in range(8, A_HEADS):
                head0(h)
            for g in (1, 2):
                unit(U_OUT0 - 3 + g, gx, hooks=({8: [mix_channels(g)]}, {8: [mix_positions(g)]}))

            def out_projection(u0, mid0, hooks):
                pe.wait_ge(acc_free, u0 - 1)
                half(2 * u0, 0, FIRST, mid, hooks=hooks[0], tile_wait=(mid_ready, mid0))
                pe.wait_ge(acc_free, u0)
                half(2 * u0 + 1, 1, FIRST, mid, hooks=hooks[1])
                half(2 * u0 + 2, 0, SECOND, mid, hooks=hooks[2], tile_wait=(mid_ready, mid0))
                half(2 * u0 + 3, 1, SECOND, mid)
                for f in (2, 3):
                    unit_in_pairs(u0 + f)
                with pe.Fori(1, 4) as i:
                    for s in range(4):
                        unit(u0 + s, mid, 4 * i)

            def unit_in_pairs(u):
                unit(u, mid)

            out_projection(U_OUT0, MID_ATT0, ({8: [mix_channels(3)]}, {8: [mix_positions(3)]}, {}))

            def hidden(u, f, k, o=0, of=0, ok=0, chunk=0):
                if u in (U_FF0, U_FF1) and isinstance(o, int):
                    n = N_FFN0 if u == U_FF0 else N_FFN1
                    unit(u, gx, tile_wait=(gx_ready, GX_BEFORE[n]), hooks=({}, {4: [stat_sum(n)]}))
                elif u in (U_FF0 + 1, U_FF1 + 1) and isinstance(o, int):
                    n = N_FFN0 if u == U_FF0 + 1 else N_FFN1
                    unit(u, gx, hooks=({4: [stat_spread(n)]}, {}))
                else:
                    unit(u, gx, o)

            def output(u, f, k, o=0, of=0, ok=0, chunk=0):
                layer = k // (FF_CHUNKS * KT)
                base = (MID_FF0, MID_FF1)[layer] + (k - f) - layer * FF_CHUNKS * KT
                unit(u, mid, o, tile_wait=(mid_ready, base + chunk) if f == 0 else None)

            feed_forward(pe, 0, U_FF0, hidden, output, output)

            unit(U_QKV1, gx, tile_wait=(gx_ready, GX_BEFORE[N_MIX1]), hooks=({}, {4: [stat_sum(N_MIX1)]}))
            unit(U_QKV1 + 1, gx, hooks=({4: [stat_spread(N_MIX1)]}, {}))

            def attend1(h, oh=0):
                def step():
                    n = A_HEADS + h
                    pe.wait_ge(v_copied, n + 1 + oh)
                    pe.wait_ge(pt_copied, n + 1 + oh)
                    for t in range(QT):
                        for kt in range(QT):
                            ins = pe.matmul(ps_o[:, t * SEQ:(t + 1) * SEQ], attn_t[:, kt, t * P:(t + 1) * P],
                                            v_tok[:, kt, :], start=kt == 0, stop=kt == QT - 1)
                    ins.then_inc(o_ready, 1)
                return step

            def turn_output(h, oh=0):
                def step():
                    pe.wait_ge(onorm_ready, QT * (h + 1) + QT * oh)
                    pe.wait_ge(mid_ready, MID_ATT1 + 2 * h + 2 * oh)
                    for j in range(2):
                        for t in range(QT):
                            ins = pe.transpose(ps_aux[:, j * SEQ + t * P:j * SEQ + (t + 1) * P],
                                               o_norm[:, t, j * P:(j + 1) * P], ident[:])
                    ins.then_inc(ot_ready, 1)
                return step

            def head1(h, oh=0):
                u, o, n = U_QKV1 + 2 + 6 * h, 6 * oh, A_HEADS + h
                p, s, read = U_OUT0 + 2 + 6 * h, A_HEADS + 2 * h, A_HEADS + 2 * h
                unit(u, gx, o, hooks=({8: [scores(0, s, p, read, 2 * oh, o, 2 * oh)]}, {}))
                unit(u + 1, gx, o)
                unit(u + 2, gx, o, hooks=({8: [scores(1, s + 1, p + 2, read, 2 * oh, o, 2 * oh)]}, {}))
                unit(u + 3, gx, o, hooks=({8: [turn_attn(n, oh)]}, {}))
                if h < C_HEADS - 1:
                    unit(u + 4, gx, o, hooks=({8: [turn_v(n, p + 4, 2, oh, o)]}, {8: [attend1(h, oh)]}))
                    unit(u + 5, gx, o, hooks=({}, {4: [turn_output(h, oh)]}))

            with pe.Fori(0, 3) as i:
                for h in range(2):
                    head1(h, 2 * i)
            head1(6)
            head1(7)
            last = C_HEADS - 1
            out_projection(U_OUT1, MID_ATT1,
                           ({8: [turn_v(HEADS - 1, U_OUT0 + 6 * C_HEADS, 2)]}, {4: [attend1(last)]},
                            {3: [turn_output(last)]}))
            feed_forward(pe, 1, U_FF1, hidden, output, output)
            stat_sum(N_FINAL)()
            stat_spread(N_FINAL)()


GX_BEFORE = {n: KT * n for n in range(N_FINAL)}


def feed_forward(eng, layer, u0, hidden, output, last_output, before_last=None):
    k0 = layer * FF_CHUNKS * KT

    def run(what, u, k, c_off, i_from, i_to):
        with eng.Fori(i_from, i_to) as i:
            for s in range(4):
                what(u + s, s, k + s, 2 * KT * c_off + 4 * i, 4 * i, KT * c_off + 4 * i, KT * c_off)

    for s in range(4):
        hidden(u0 + s, s, k0 + s)
    run(hidden, u0, k0, 0, 1, KT // 4)
    run(output, u0 + KT, k0, 0, 0, KT // 4)
    with eng.Fori(0, FF_CHUNKS - 2) as c:
        run(hidden, u0 + 2 * KT, k0 + KT, c, 0, KT // 4)
        run(output, u0 + 3 * KT, k0 + KT, c, 0, KT // 4)
    u, k = u0 + 2 * KT * (FF_CHUNKS - 1), k0 + KT * (FF_CHUNKS - 1)
    run(hidden, u, k, 0, 0, KT // 4)
    if before_last is not None:
        before_last()
    tail = 4 if layer == 1 else 0
    run(last_output, u + KT, k, 0, 0, (KT - tail) // 4)
    for s in range(KT - tail, KT):
        last_output(u + KT + s, s, k + s)


def stream_units(w_in, w_out0, ff1, ff2, w_qkv, w_out1):
    def tiles(w):
        return w.reshape(w.shape[0] // P, P, w.shape[1] // P, P).transpose(2, 1, 0, 3)

    def by_halves(w):
        t = tiles(w)
        a, b = t[0], t[1]
        h = KT // 2
        pair = np.stack([np.concatenate([a[:, :h], b[:, :h]], axis=1), np.concatenate([a[:, h:], b[:, h:]], axis=1)])
        return np.concatenate([pair, t[2:]])

    def mlp(w1, w2):
        up, down = tiles(w1), tiles(w2)
        parts = []
        for c in range(FF_CHUNKS):
            parts += [up[c * KT:(c + 1) * KT], down[:, :, c * KT:(c + 1) * KT]]
        return parts

    t = tiles(w_in)
    order0 = [x for h in range(A_HEADS) for x in (h, A_HEADS + h, 2 * A_HEADS + h)]
    order0 += [3 * A_HEADS + g for g in range(GROUPS)]
    q = tiles(w_qkv)
    n = 2 * C_HEADS
    order1 = [x for h in range(C_HEADS)
              for x in (2 * h, n + 2 * h, 2 * h + 1, n + 2 * h + 1, 2 * n + 2 * h, 2 * n + 2 * h + 1)]
    parts = [t[order0], by_halves(w_out0), *mlp(ff1[0], ff2[0]), q[order1], by_halves(w_out1), *mlp(ff1[1], ff2[1])]
    return np.concatenate(parts).reshape(UNITS, P, KT * P)


def shape_constants():
    d = np.arange(-(SEQ - 1), SEQ)
    n = np.abs(d)
    max_exact = BUCKETS // 4
    large = max_exact + (np.log(np.maximum(n, 1).astype(np.float32) / np.float32(max_exact)).astype(np.float32)
                         / np.float32(math.log(1024 / max_exact)) * np.float32(BUCKETS // 2 - max_exact)
                         ).astype(np.int32)
    bucket = np.where(d > 0, BUCKETS // 2, 0) + np.where(n < max_exact, n, np.minimum(large, BUCKETS // 2 - 1))
    onehot = np.zeros((BUCKETS + 1, LINE), np.float32)
    onehot[bucket, np.arange(d.size)] = 1.0
    reach = sum(((n % dil == 0) & (n <= window // 2)).astype(int) for window, dil in ((128, 1), (512, 4), (2048, 16)))
    onehot[BUCKETS, :d.size] = np.where(reach > 0, np.log(np.maximum(reach, 1)), -1e30)
    a_head_row = np.zeros((1, HEADS), np.float32)
    a_head_row[0, :A_HEADS] = 1.0
    c = np.arange(P)
    angle = 2 * np.pi * (np.outer(c, c) % P) / P
    channel = np.stack([np.cos(angle), np.sin(angle)], axis=1).astype(np.float32)
    s = np.arange(SEQ)
    angle = (2 * np.pi * (np.outer(s, s) % SEQ) / SEQ).reshape(QT, P, SEQ).transpose(1, 0, 2)
    position = (np.stack([np.cos(angle), -np.sin(angle)], axis=2) / math.sqrt(SEQ * P)).astype(np.float32)
    return onehot, a_head_row, channel, position, np.eye(P, dtype=np.float32)


def kernel(x, norm_mix_g, norm_ffn_g, norm_final_g, rel_bias_table, w_in_even, w_fnet, w_out_even, w_qkv_odd,
           lambda_q1, lambda_k1, lambda_q2, lambda_k2, subln_g, w_out_odd, w_ff1, w_ff2):
    import concourse.bacc as bacc
    from concourse.bass_utils import run_bass_kernel_spmd

    onehot, a_head_row, channel, position, identity = shape_constants()
    gains = np.stack([norm_mix_g[0], norm_ffn_g[0], norm_mix_g[1], norm_ffn_g[1], norm_final_g])
    arrays = {
        "xT": np.ascontiguousarray(np.asarray(x)[0].T),
        "weights": stream_units(*(np.asarray(a) for a in (w_in_even[0], w_out_even[0], w_ff1, w_ff2, w_qkv_odd[0],
                                                          w_out_odd[0]))),
        "gains": np.ascontiguousarray(gains.reshape(5, KT, P).transpose(2, 0, 1)),
        "subln": np.ascontiguousarray(np.asarray(subln_g)[0].reshape(2, P).T),
        "lambdas": np.ascontiguousarray(np.concatenate([lambda_q1, lambda_k1, lambda_q2, lambda_k2]).T),
        "table": np.ascontiguousarray(rel_bias_table),
        "w_fnet": np.ascontiguousarray(np.asarray(w_fnet)[0]),
        "onehot": onehot, "a_head_row": a_head_row, "channel_dft": channel, "position_dft": position,
        "identity": identity,
    }
    nc = bacc.Bacc("TRN2", target_bir_lowering=False, num_devices=1)
    aps = {name: nc.dram_tensor(f"{name}_dram", a.shape, mybir.dt.from_np(a.dtype), kind="ExternalInput").ap()
           for name, a in arrays.items()}
    out = nc.dram_tensor("out_dram", (D, SEQ), F32, kind="ExternalOutput").ap()
    trunk(nc, outT=out, **aps)
    result = run_bass_kernel_spmd(nc, [{f"{name}_dram": a for name, a in arrays.items()}], core_ids=[0])
    return np.ascontiguousarray(result.results[0]["out_dram"].T)[None]
```

```python
from contextlib import ExitStack
import math

import numpy as np
import concourse.bass as bass
from concourse import mybir

F32 = mybir.dt.float32
F32R = mybir.dt.float32r
ALU = mybir.AluOpType
ACT = mybir.ActivationFunctionType
AX_X = mybir.AxisListType.X

P = 128
D = 2048
SEQ = 256
KT = D // P
QT = SEQ // P
A_HEADS, GROUPS, C_HEADS = 12, 4, 8
HEADS = A_HEADS + C_HEADS
BUCKETS = 32
FF_CHUNKS = 4
EPS = 1e-6
SCALE = 1.0 / math.sqrt(P)
LAMBDA_INIT = 0.8 - 0.6 * math.exp(-0.3 * 1)
LINE = 2 * SEQ

HALF = KT // 2 * P
RAW_SLOTS = 4
RING = 4

U_QKV0 = 0
U_OUT0 = U_QKV0 + 3 * A_HEADS + GROUPS
U_FF0 = U_OUT0 + KT
U_QKV1 = U_FF0 + 2 * KT * FF_CHUNKS
U_OUT1 = U_QKV1 + 6 * C_HEADS
U_FF1 = U_OUT1 + KT
UNITS = U_FF1 + 2 * KT * FF_CHUNKS

MID_ATT0, MID_FF0 = 0, KT
MID_ATT1 = MID_FF0 + KT * FF_CHUNKS
MID_FF1 = MID_ATT1 + KT

COPIES_QKV0, COPIES_FF0 = 0, U_OUT0
COPIES_QKV1 = COPIES_FF0 + KT * FF_CHUNKS
COPIES_FF1 = COPIES_QKV1 + 6 * C_HEADS

N_MIX0, N_FFN0, N_MIX1, N_FFN1, N_FINAL = range(5)
SUMS_BEFORE = {n: (KT + 1) * (n - 1) for n in range(1, 6)}
SQUARES_BEFORE = {n: KT * (n - 1) for n in range(1, 5)}
BIAS_FIRST = A_HEADS - KT // QT


def trunk(nc, xT, weights, gains, subln, lambdas, table, w_fnet, onehot, a_head_row, channel_dft,
          position_dft, identity, outT):
    ctx = ExitStack()
    with ctx:
        def sb(name, shape, dt=F32):
            return ctx.enter_context(nc.sbuf_tensor(name, shape, dt))

        def pb(name, shape):
            return ctx.enter_context(nc.psum_tensor(name, shape, F32))

        def sem(name):
            return ctx.enter_context(nc.semaphore(name))

        x = sb("x", [P, KT, SEQ])
        gx = sb("gx", [P, KT, 2 * SEQ], F32R)
        mid = sb("mid", [P, KT, 2 * SEQ], F32R)
        raw = sb("raw", [P, RAW_SLOTS, 2 * HALF])
        w_hi = sb("w_hi", [P, RING, HALF], F32R)
        w_lo = sb("w_lo", [P, RING, HALF], F32R)
        bias = sb("bias", [P, A_HEADS, QT, SEQ])
        y_out = bias[:].rearrange("p h t k -> p (h t k)")[:, 0:KT * SEQ].rearrange(
            "p (f t) -> p f t", f=KT)
        x0_sq = bias[:, BIAS_FIRST:A_HEADS, :, :].rearrange("p h t k -> p (h t) k")
        line = bias[0:HEADS, 0, :, :].rearrange("h t k -> h (t k)")
        one_hot = bias[0:BUCKETS + 1, 1, :, :].rearrange("b t k -> b (t k)")
        gain = sb("gain", [P, 5, KT])
        sub_gain = sb("sub_gain", [P, 2])
        sub_gain_in = sb("sub_gain_in", [P, 2])
        lam_in = sb("lam_in", [P, 4])
        lam_prod = sb("lam_prod", [P, 2])
        lam_exp = sb("lam_exp", [P, 2])
        lam_diff = sb("lam_diff", [P, 1])
        neg_lam = sb("neg_lam", [P, 1])
        tab = sb("tab", [BUCKETS + 1, HEADS])
        wf = sb("wf", [P, GROUPS, P])
        ch_dft = sb("ch_dft", [P, 2, P])
        pos_dft = sb("pos_dft", [P, QT, 2, SEQ])
        ch_map = sb("ch_map", [P, GROUPS, 2, P])
        mixed = sb("mixed", [P, QT, 2 * P])
        ident = sb("ident", [P, P])
        ones = sb("ones", [P, P])
        minus_half = sb("minus_half", [P, 2])
        copied = sb("copied", [P, SEQ])
        summed = sb("summed", [P, SEQ])
        relu = sb("relu", [P, SEQ])
        square = sb("square", [P, SEQ])
        x_sq = sb("x_sq", [P, SEQ])
        sum_sq = sb("sum_sq", [P, SEQ])
        rstd = sb("rstd", [P, SEQ])
        mean_sq = sb("mean_sq", [P, QT])
        rstd_col = sb("rstd_col", [P, QT])
        diag = sb("diag", [P, QT, P])
        q_t = sb("q_t", [P, 2, SEQ])
        u_t = q_t[:, 1, :]
        k_t = sb("k_t", [P, 2, SEQ])
        v_t = sb("v_t", [P, 2, SEQ])
        v_tok = sb("v_tok", [P, QT, 2 * P])
        logits = sb("logits", [P, 2, QT, SEQ])
        probs = logits
        row_max = sb("row_max", [P, 2, QT])
        neg_max = sb("neg_max", [P, 2, QT])
        row_sum = sb("row_sum", [P, 2, QT])
        row_inv = sb("row_inv", [P, 2, QT])
        lam_inv = sb("lam_inv", [P, QT])
        part0, o_norm = pos_dft[:, 0, :, :], pos_dft[:, 1, :, :]
        attn = sb("attn", [P, QT, SEQ])
        attn_t = sb("attn_t", [P, QT, SEQ])
        o_sq = mixed
        o_sum = sb("o_sum", [P, QT])
        o_mean = sb("o_mean", [P, QT])
        o_inv = sb("o_inv", [P, QT])

        acc = [pb(f"acc{i}", [P, 2 * SEQ]) for i in range(2)]
        ps_scores = [pb(f"ps_scores{i}", [P, QT, SEQ]) for i in range(2)]
        ps_attn_t = pb("ps_attn_t", [P, QT, SEQ])
        ps_v = pb("ps_v", [P, QT, 2 * P])
        ps_o = pb("ps_o", [P, 2 * SEQ])
        ps_aux = pb("ps_aux", [P, 2 * SEQ])

        bias_line = nc.dram_tensor("bias_line", (HEADS, LINE), F32, kind="Internal").ap()

        raw_landed = [sem(f"raw_landed{i}") for i in range(RAW_SLOTS)]
        hi_ready, lo_ready = sem("hi_ready"), sem("lo_ready")
        w_used = sem("w_used")
        acc_free = sem("acc_free")
        acc_half = sem("acc_half")
        copy_ready = sem("copy_ready")
        proj_ready = sem("proj_ready")
        relu_done, squared = sem("relu_done"), sem("squared")
        mid_hi, mid_ready = sem("mid_hi"), sem("mid_ready")
        gx_hi, gx_ready = sem("gx_hi"), sem("gx_ready")
        xsq_done, sum_steps = sem("xsq_done"), sem("sum_steps")
        stat_ready, mean_ready = sem("stat_ready"), sem("mean_ready")
        inv_ready, diag_ready = sem("inv_ready"), sem("diag_ready")
        bcast_ready, rstd_ready = sem("bcast_ready"), sem("rstd_ready")
        scores_ready, scores_read = sem("scores_ready"), sem("scores_read")
        max_done, neg_ready, exp_done = sem("max_done"), sem("neg_ready"), sem("exp_done")
        soft_steps, attn_ready = sem("soft_steps"), sem("attn_ready")
        vt_ready, pt_ready = sem("vt_ready"), sem("pt_ready")
        v_copied, pt_copied, o_ready = sem("v_copied"), sem("pt_copied"), sem("o_ready")
        osq_done, omean_ready = sem("osq_done"), sem("omean_ready")
        oinv_ready, onorm_ready, ot_ready = sem("oinv_ready"), sem("onorm_ready"), sem("ot_ready")
        mix1_ready, mix_copied, mix2_ready = sem("mix1_ready"), sem("mix_copied"), sem("mix2_ready")
        x_landed = [sem(f"x_landed{i}") for i in range(4)]
        small_landed, tab_landed, dft_landed = sem("small_landed"), sem("tab_landed"), sem("dft_landed")
        gain_landed, ones_ready = sem("gain_landed"), sem("ones_ready")
        map_ready, map_copied = sem("map_ready"), sem("map_copied")
        line_ready, line_copied, line_stored = sem("line_ready"), sem("line_copied"), sem("line_stored")
        bias_first, bias_rest, bias_second = sem("bias_first"), sem("bias_rest"), sem("bias_second")
        x0_squared, x0_summed = sem("x0_squared"), sem("x0_summed")
        lam_steps, lam_sum_ready, lam_exp_ready = sem("lam_steps"), sem("lam_sum_ready"), sem("lam_exp_ready")
        y_last_ready, y_ready, y_stored = sem("y_last_ready"), sem("y_ready"), sem("y_stored")

        def acc_of(u):
            return ps_scores[1][:].rearrange("p t k -> p (t k)") if u == 2 else acc[u % 2][:]

        def load_bias(eng, landed, line_head, first, last):
            for t in range(QT):
                src = bass.AP(bias_line.tensor, line_head * LINE + P * t, [[1, P], [LINE, last - first], [1, SEQ]])
                eng.dma_start(bias[:, first:last, t, :], src).then_inc(landed, 16)

        block = ctx.enter_context(nc.Block())

        @block.sync
        def _(sp):
            def load(u, o=0, free=True):
                slot = u % RAW_SLOTS
                if free:
                    sp.wait_ge(lo_ready, 2 * (u - RAW_SLOTS + 1) + 2 * o)
                sp.dma_start(raw[:, slot, :], weights[u + o]).then_inc(raw_landed[slot], 16)

            def load_x(g):
                sp.dma_start(x[:, 4 * g:4 * g + 4, :], xT.rearrange("(f p) t -> p f t", p=P)[:, 4 * g:4 * g + 4, :]
                             ).then_inc(x_landed[g], 16)

            load(0, free=False)
            sp.dma_start(gain[:], gains).then_inc(gain_landed, 16)
            for g in range(4):
                load_x(g)
            load(1, free=False)
            sp.wait_ge(line_copied, 1)
            sp.dma_start(bias_line, line).then_inc(line_stored, 16)
            load(2, free=False)
            sp.wait_ge(line_stored, 16)
            load_bias(sp, bias_first, 0, 0, BIAS_FIRST)
            load(3, free=False)
            sp.wait_ge(stat_ready, 1)
            load_bias(sp, bias_rest, BIAS_FIRST, BIAS_FIRST, A_HEADS)
            with sp.Fori(0, UNITS // RAW_SLOTS - 1) as i:
                for s in range(RAW_SLOTS):
                    load(RAW_SLOTS + s, RAW_SLOTS * i)
            for g in (0, 3, 1, 2):
                sp.wait_ge(*((y_last_ready, 1) if g == 3 else (y_ready, g + 1)))
                sp.dma_start(outT.rearrange("(f p) t -> p f t", p=P)[:, 4 * g:4 * g + 4, :],
                             y_out[:, 4 * g:4 * g + 4, :]).then_inc(y_stored, 16)
            sp.wait_ge(y_stored, 16 * 4)

        @block.gpsimd
        def _(pool):
            pool.memset(ones[:], 1.0)
            pool.memset(minus_half[:], -0.5).then_inc(ones_ready, 1)
            for g in range(4):
                pool.wait_ge(x_landed[g], 16)
                tiles = slice(4 * g, 4 * g + 4)
                pool.tensor_tensor(x0_sq[:, tiles, :], x[:, tiles, :], x[:, tiles, :], ALU.mult).then_inc(x0_squared, 1)
            pool.dma_start(wf[:], w_fnet.rearrange("g c e -> c g e")).then_inc(dft_landed, 16)
            pool.dma_start(ch_dft[:], channel_dft).then_inc(dft_landed, 16)
            pool.dma_start(pos_dft[:], position_dft).then_inc(dft_landed, 16)
            pool.wait_ge(ones_ready, 1)

            def token_inverse(n):
                pool.wait_ge(mean_ready, n + 1)
                pool.tensor_tensor(rstd_col[:], mean_sq[:], minus_half[:], ALU.pow).then_inc(inv_ready, 1)

            token_inverse(N_MIX0)
            token_inverse(N_FFN0)
            token_inverse(N_MIX1)
            with pool.Fori(0, C_HEADS) as h:
                pool.wait_ge(omean_ready, h + 1)
                pool.tensor_tensor(o_inv[:], o_mean[:], minus_half[:], ALU.pow).then_inc(oinv_ready, 1)
            token_inverse(N_FFN1)
            token_inverse(N_FINAL)
            pool.wait_ge(rstd_ready, N_FINAL + 1)
            for f in range(12, 16):
                ins = pool.tensor_tensor(y_out[:, f, :], y_out[:, f, :], rstd[:], ALU.mult)
            ins.then_inc(y_last_ready, 1)

        @block.scalar
        def _(act):
            def split_hi(n, o=0):
                u, part = n // 2, n % 2
                if part == 0:
                    act.wait_ge(raw_landed[u % RAW_SLOTS], 16 * (u // RAW_SLOTS + 1) + 16 // RAW_SLOTS * o)
                if n >= RING:
                    act.wait_ge(w_used, n - RING + 1 + 2 * o)
                act.activation(w_hi[:, n % RING, :], raw[:, u % RAW_SLOTS, part * HALF:(part + 1) * HALF],
                               ACT.Copy).then_inc(hi_ready, 1)

            def copy_cross(u, o):
                act.wait_ge(w_used, 2 * u + 2 + 2 * o)
                act.wait_ge(acc_free, u + o)
                act.activation(copied[:], acc_of(u)[:, SEQ:], ACT.Copy).then_inc(copy_ready, 1)

            def unit(u, o=0, before=(), first=(), second=(), copy=True, split=True):
                for step in before:
                    step()
                if split:
                    split_hi(2 * u + 4, o)
                for step in first:
                    step()
                if copy:
                    copy_cross(u, o)
                if split:
                    split_hi(2 * u + 5, o)
                for step in second:
                    step()

            def hi_gx(n, t):
                dst = y_out[:, t, :] if n == N_FINAL else gx[:, t, 0:SEQ]
                act.activation(dst, x[:, t, :], ACT.Copy, scale=gain[:, n, bass.ts(t, 1)]).then_inc(gx_hi, 1)

            def gx_part(n, f, of=0):
                t = f + of
                act.wait_ge(sum_steps, SUMS_BEFORE[n] + 1 + t)
                hi_gx(n, t)
                act.activation(x_sq[:], x[:, t, :], ACT.Square).then_inc(xsq_done, 1)

            def residual(n, u, f, o=0, of=0):
                def step():
                    act.wait_ge(acc_free, u + 1 + o)
                    gx_part(n, f, of)
                return step

            def exps(m, s, head, heads_before, os=0, oh=0):
                def step():
                    act.wait_ge(neg_ready, s + 1 + os)
                    act.wait_ge(attn_ready, QT * (heads_before + oh))
                    for t in range(QT):
                        act.activation(probs[:, m, t, :], logits[:, m, t, :], ACT.Exp,
                                       bias=neg_max[:, m, t:t + 1],
                                       accum_out=row_sum[:, m, t:t + 1]).then_inc(exp_done, 1)
                return step

            def copy_v(n, width, oh=0):
                def step():
                    act.wait_ge(vt_ready, n + 1 + oh)
                    act.wait_ge(o_ready, n + oh)
                    act.activation(v_tok[:, :, 0:width], ps_v[:, :, 0:width], ACT.Copy).then_inc(v_copied, 1)
                return step

            def copy_attn(n, oh=0):
                def step():
                    act.wait_ge(pt_ready, n + 1 + oh)
                    act.wait_ge(o_ready, n + oh)
                    act.activation(attn_t[:], ps_attn_t[:, :, ::-1], ACT.Copy).then_inc(pt_copied, 1)
                return step

            act.dma_start(tab[0:BUCKETS, :], table).then_inc(tab_landed, 16)
            act.dma_start(tab[BUCKETS:BUCKETS + 1, :], a_head_row).then_inc(tab_landed, 16)
            act.dma_start(one_hot, onehot).then_inc(tab_landed, 16)
            act.dma_start(ident[:], identity).then_inc(small_landed, 16)
            act.dma_start(lam_in[:], lambdas).then_inc(small_landed, 16)
            act.dma_start(sub_gain_in[:], subln).then_inc(small_landed, 16)
            split_hi(0)
            act.wait_ge(gain_landed, 16)
            for f in range(KT):
                act.wait_ge(x_landed[f // 4], 16)
                hi_gx(N_MIX0, f)
                if f == 3:
                    split_hi(1)
                if f == 11:
                    act.wait_ge(line_ready, 1)
                    act.activation(line, ps_scores[0][0:HEADS, :, :].rearrange("h t k -> h (t k)"), ACT.Copy
                                   ).then_inc(line_copied, 1)
            split_hi(2)
            split_hi(3)
            split_hi(4)
            split_hi(5)
            copy_cross(0, 0)
            split_hi(6)
            split_hi(7)
            copy_cross(1, 0)

            def copy_maps():
                act.wait_ge(map_ready, 1)
                act.activation(ch_map[:, :, 0, :], ps_o[:].rearrange("p (g e) -> p g e", g=GROUPS), ACT.Copy)
                act.activation(ch_map[:, :, 1, :], ps_attn_t[:].rearrange("p t (g e) -> p (t g) e", e=P), ACT.Copy
                               ).then_inc(map_copied, 1)
                act.wait_ge(lam_sum_ready, 1)
                act.activation(lam_exp[:], ps_v[:, 0, 0:2], ACT.Exp).then_inc(lam_exp_ready, 1)

            def hi_att0(h, oh):
                def step():
                    act.wait_ge(o_ready, h + 1 + oh)
                    act.activation(mid[:, h + oh, 0:SEQ], ps_o[:, 0:SEQ], ACT.Copy).then_inc(mid_hi, 1)
                return step

            def copy_mixed(g):
                def step():
                    act.wait_ge(mix1_ready, g + 1)
                    act.wait_ge(mix2_ready, g)
                    act.activation(mixed[:], ps_scores[1][:], ACT.Copy).then_inc(mix_copied, 1)
                return step

            def hi_mix(g):
                def step():
                    act.wait_ge(mix2_ready, g + 1)
                    act.activation(mid[:, A_HEADS + g, 0:SEQ], ps_aux[:, 0:SEQ], ACT.Copy).then_inc(mid_hi, 1)
                return step

            def head0(h, oh=0):
                u, o = 2 + 3 * h, 3 * oh
                if h == 0:
                    unit(u, second=[copy_maps, exps(0, 0, 0, 0)])
                else:
                    unit(u, o, first=[exps(0, h, h, h, oh, oh)])
                unit(u + 1, o, second=[copy_v(h, P, oh), copy_attn(h, oh)])
                if h < A_HEADS - 1:
                    unit(u + 2, o, first=[hi_att0(h, oh)])
                else:
                    unit(u + 2, o, first=[hi_att0(h, oh), copy_mixed(0)], second=[hi_mix(0)])

            head0(0)
            with act.Fori(0, 2) as i:
                for h in range(1, 5):
                    head0(h, 4 * i)
            for h in range(9, A_HEADS):
                head0(h)
            for g in (1, 2):
                unit(U_OUT0 - 3 + g, first=[copy_mixed(g)], second=[hi_mix(g)])

            def out_projection(u0, n, before=(), first=(), second=()):
                for step in before:
                    step()
                split_hi(2 * u0 + 4)
                for step in first:
                    step()
                split_hi(2 * u0 + 5)
                for step in second:
                    step()
                split_hi(2 * u0 + 6)
                residual(n, u0, 0)()
                split_hi(2 * u0 + 7)
                residual(n, u0 + 1, 1)()
                for f in (2, 3):
                    unit(u0 + f, copy=False, second=[residual(n, u0 + f, f)])
                with act.Fori(1, 4) as i:
                    for s in range(4):
                        unit(u0 + s, 4 * i, copy=False, second=[residual(n, u0 + s, s, 4 * i, 4 * i)])

            out_projection(U_OUT0, N_FFN0, first=[copy_mixed(3)], second=[hi_mix(3)])
            load_bias(act, bias_second, A_HEADS, 0, C_HEADS)

            def hidden(u, f, k, o=0, of=0, ok=0, chunk=0):
                def hi_hidden():
                    act.wait_ge(squared, k + 1 + ok)
                    act.activation(mid[:, f + of, 0:SEQ], square[:], ACT.Copy).then_inc(mid_hi, 1)
                unit(u, o, second=[hi_hidden])

            def output(u, f, k, o=0, of=0, ok=0, chunk=0):
                unit(u, o, copy=False)

            def last_output(n):
                def run(u, f, k, o=0, of=0, ok=0, chunk=0):
                    unit(u, o, copy=False, second=[residual(n, u, f, o, of)], split=u + 2 < UNITS)
                return run

            feed_forward(act, 0, U_FF0, hidden, output, last_output(N_MIX1))

            unit(U_QKV1)
            unit(U_QKV1 + 1)

            def squares(h, oh=0):
                def step():
                    act.wait_ge(o_ready, A_HEADS + h + 1 + oh)
                    act.wait_ge(osq_done, QT * (h + oh))
                    for t in range(QT):
                        act.activation(o_sq[:, t, :], ps_o[:, t * SEQ:(t + 1) * SEQ], ACT.Square,
                                       accum_out=o_sum[:, t:t + 1]).then_inc(osq_done, 1)
                return step

            def hi_att1(h, oh=0):
                def step():
                    act.wait_ge(ot_ready, h + 1 + oh)
                    for j in range(2):
                        act.activation(mid[:, 2 * h + j + 2 * oh, 0:SEQ], ps_aux[:, j * SEQ:(j + 1) * SEQ], ACT.Copy,
                                       scale=sub_gain[:, j:j + 1]).then_inc(mid_hi, 1)
                return step

            def head1(h, oh=0):
                u, o, g = U_QKV1 + 2 + 6 * h, 6 * oh, A_HEADS + h
                unit(u, o, first=[exps(0, A_HEADS + 2 * h, h, g, 2 * oh, oh)])
                unit(u + 1, o)
                unit(u + 2, o, first=[exps(1, A_HEADS + 2 * h + 1, h, g, 2 * oh, oh)])
                unit(u + 3, o, second=[copy_attn(g, oh)])
                if h < C_HEADS - 1:
                    unit(u + 4, o, first=[copy_v(g, 2 * P, oh)])
                    unit(u + 5, o, before=[squares(h, oh)], second=[hi_att1(h, oh)])

            head1(0)
            with act.Fori(0, 3) as i:
                for h in (1, 2):
                    head1(h, 2 * i)
            head1(7)
            out_projection(U_OUT1, N_FFN1, before=[copy_v(HEADS - 1, 2 * P)], first=[squares(C_HEADS - 1)],
                           second=[hi_att1(C_HEADS - 1)])
            feed_forward(act, 1, U_FF1, hidden, output, last_output(N_FINAL))

        @block.vector
        def _(dve):
            def split_lo(n, o=0):
                u, part = n // 2, n % 2
                dve.wait_ge(hi_ready, n + 1 + 2 * o)
                dve.tensor_tensor(w_lo[:, n % RING, :], raw[:, u % RAW_SLOTS, part * HALF:(part + 1) * HALF],
                                  w_hi[:, n % RING, :].bitcast(F32), ALU.subtract).then_inc(lo_ready, 1)

            def sum_product(u, c, o=0, oc=0):
                dve.wait_ge(copy_ready, c + 1 + oc)
                dve.tensor_tensor(summed[:], acc_of(u)[:, 0:SEQ], copied[:], ALU.add).then_inc(acc_free, 1)
                dve.wait_ge(acc_free, u + 1 + o)

            def projected(u, c, dst, scale=1.0, o=0, oc=0):
                def step():
                    p = c if u < U_OUT0 else c - FF_CHUNKS * KT
                    dve.wait_ge(proj_ready, p + oc)
                    sum_product(u, c, o, oc)
                    dve.scalar_tensor_tensor(dst, summed[:], scale, rstd[:], ALU.mult, ALU.mult
                                             ).then_inc(proj_ready, 1)
                return step

            def add_to_residual(u, f, r, o=0, of=0, r_o=0, late=0):
                def step():
                    t = f + of
                    dve.wait_ge(w_used, 2 * u + 2 + late + 2 * o)
                    dve.tensor_tensor(x[:, t, :], x[:, t, :], acc_of(u)[:, 0:SEQ], ALU.add).then_inc(acc_half, 1)
                    dve.wait_ge(acc_half, r + 1 + r_o)
                    dve.tensor_tensor(x[:, t, :], x[:, t, :], acc_of(u)[:, SEQ:], ALU.add).then_inc(acc_free, 1)
                return step

            def lo_gx(n, t):
                dve.wait_ge(gx_hi, KT * n + t + 1)
                dve.scalar_tensor_tensor(gx[:, t, SEQ:], x[:, t, :], gain[:, n, bass.ts(t, 1)],
                                         gx[:, t, 0:SEQ].bitcast(F32), ALU.mult, ALU.subtract).then_inc(gx_ready, 1)

            def gx_rest(n, f, of=0):
                def step():
                    t = f + of
                    if n != N_FINAL:
                        lo_gx(n, t)
                    dve.wait_ge(xsq_done, SQUARES_BEFORE[n] + t + 1)
                    dve.wait_ge(sum_steps, SUMS_BEFORE[n] + 1 + t)
                    dve.tensor_tensor(sum_sq[:], sum_sq[:], x_sq[:], ALU.add).then_inc(sum_steps, 1)
                return step

            def clear_sum():
                dve.memset(sum_sq[:], 0.0).then_inc(sum_steps, 1)

            def unit(u, evac, o=0, before=(), first=(), mid_steps=(), second=(), split=True):
                for step in before:
                    step()
                if split:
                    split_lo(2 * u + 4, o)
                for step in first:
                    step()
                evac()
                if split:
                    split_lo(2 * u + 5, o)
                for step in second:
                    step()

            def token_stats(n):
                dve.wait_ge(stat_ready, n + 1)
                dve.tensor_scalar(mean_sq[:], ps_aux[:, 0:QT], 1.0 / D, EPS, ALU.mult, ALU.add
                                  ).then_inc(mean_ready, 1)
                dve.wait_ge(inv_ready, n + 1)
                for t in range(QT):
                    dve.tensor_scalar(diag[:, t, :], ident[:], rstd_col[:, t:t + 1], None, ALU.mult
                                      ).then_inc(diag_ready, 1)

            def token_rstd(n):
                dve.wait_ge(bcast_ready, n + 1)
                dve.tensor_copy(rstd[:], ps_aux[:, 0:SEQ]).then_inc(rstd_ready, 1)
                dve.wait_ge(rstd_ready, n + 1)

            def first_unit(u, n, evac, second=()):
                split_lo(2 * u + 4)
                token_stats(n)
                split_lo(2 * u + 5)
                token_rstd(n)
                evac()
                for step in second:
                    step()

            def score_rows(m, s, before, head, os=0, ob=0, oh=0):
                def step():
                    dve.wait_ge(scores_ready, s + 1 + os)
                    dve.wait_ge(exp_done, before + ob)
                    dve.tensor_tensor(logits[:, m, :, :], ps_scores[m][:], bias[:, head + oh, :, :], ALU.add
                                      ).then_inc(scores_read, 1)
                    dve.wait_ge(scores_read, s + 1 + os)
                    dve.tensor_reduce(row_max[:, m, :], logits[:, m, :, :], AX_X, ALU.max).then_inc(max_done, 1)
                    dve.wait_ge(max_done, s + 1 + os)
                    dve.tensor_scalar(neg_max[:, m, :], row_max[:, m, :], -1.0, None, ALU.mult
                                      ).then_inc(neg_ready, 1)
                return step

            split_lo(0)
            dve.wait_ge(gain_landed, 16)
            for f in range(KT):
                dve.wait_ge(x_landed[f // 4], 16)
                lo_gx(N_MIX0, f)
                if f == 3:
                    split_lo(1)
            split_lo(2)
            split_lo(3)
            dve.wait_ge(small_landed, 16 * 3)
            dve.tensor_tensor(lam_prod[:], lam_in[:, 0:4:2], lam_in[:, 1:4:2], ALU.mult).then_inc(lam_steps, 1)
            dve.tensor_scalar(sub_gain[:], sub_gain_in[:], 1.0 - LAMBDA_INIT, None, ALU.mult).then_inc(lam_steps, 1)
            dve.wait_ge(x0_squared, 4)
            n, steps = KT, 0
            while n > 1:
                n //= 2
                dst = x0_sq[:, 0:n, :] if n > 1 else sum_sq[:]
                a, b = (x0_sq[:, k * n:(k + 1) * n, :] for k in range(2))
                if n == 1:
                    a, b = x0_sq[:, 0, :], x0_sq[:, 1, :]
                dve.wait_ge(x0_summed, steps)
                dve.tensor_tensor(dst, a, b, ALU.add).then_inc(x0_summed, 1)
                steps += 1

            def negative_lambda():
                dve.wait_ge(lam_exp_ready, 1)
                dve.tensor_tensor(lam_diff[:], lam_exp[:, 1:2], lam_exp[:, 0:1], ALU.subtract).then_inc(lam_steps, 1)
                dve.wait_ge(lam_steps, 3)
                dve.tensor_scalar(neg_lam[:], lam_diff[:], -LAMBDA_INIT, None, ALU.add).then_inc(lam_steps, 1)

            q0, k0, v0 = q_t[:, 0, ::-1], k_t[:, 0, :], v_t[:, 0, :]
            split_lo(4)
            token_stats(N_MIX0)
            split_lo(5)
            split_lo(6)
            token_rstd(N_MIX0)
            projected(0, 0, q0, SCALE)()
            split_lo(7)
            projected(1, 1, k0)()

            def normalise(h, oh=0):
                def step():
                    dve.wait_ge(exp_done, QT * (h + 1) + QT * oh)
                    dve.wait_ge(attn_ready, QT * (h + oh))
                    dve.reciprocal(row_inv[:, 0, :], row_sum[:, 0, :]).then_inc(soft_steps, 1)
                    dve.wait_ge(soft_steps, h + 1 + oh)
                    dve.wait_ge(pt_ready, h + oh)
                    for t in range(QT):
                        dve.tensor_scalar(attn[:, t, :], probs[:, 0, t, :], row_inv[:, 0, t:t + 1], None, ALU.mult
                                          ).then_inc(attn_ready, 1)
                return step

            def lo_part(tile, src, ot=0):
                def step():
                    dve.wait_ge(mid_hi, tile + 1 + ot)
                    dve.tensor_tensor(mid[:, tile + ot, SEQ:], src, mid[:, tile + ot, 0:SEQ].bitcast(F32),
                                      ALU.subtract).then_inc(mid_ready, 1)
                return step

            def head0(h, oh=0):
                u, o = 2 + 3 * h, 3 * oh
                last = h == A_HEADS - 1
                if h == 0:
                    unit(u, projected(u, u, v0),
                         second=[lambda: dve.wait_ge(bias_first, 16 * QT), score_rows(0, 0, 0, 0), normalise(0)])
                else:
                    unit(u, projected(u, u, v0, 1.0, o, o), o,
                         first=[score_rows(0, h, QT * h, h, oh, QT * oh, oh), normalise(h, oh)])
                unit(u + 1, projected(u + 1, u + 1, u_t if last else q0, 1.0 if last else SCALE, o, o), o)
                unit(u + 2, projected(u + 2, u + 2, u_t if last else k0, 1.0, o, o), o,
                     first=[lo_part(h, ps_o[:, 0:SEQ], oh)],
                     second=[lo_part(A_HEADS, ps_aux[:, 0:SEQ])] if last else [])

            head0(0)
            negative_lambda()
            dve.wait_ge(bias_rest, 16 * QT)
            with dve.Fori(0, 2) as i:
                for h in range(1, 5):
                    head0(h, 4 * i)
            for h in range(9, A_HEADS):
                head0(h)
            for g in (1, 2):
                u = U_OUT0 - 3 + g
                unit(u, projected(u, u, u_t), second=[lo_part(A_HEADS + g, ps_aux[:, 0:SEQ])])

            def out_projection(u0, n, r, first=(), second=()):
                clear_sum()
                split_lo(2 * u0 + 4)
                for step in first:
                    step()
                split_lo(2 * u0 + 5)
                for step in second:
                    step()
                add_to_residual(u0, 0, r, late=1)()
                split_lo(2 * u0 + 6)
                gx_rest(n, 0)()
                add_to_residual(u0 + 1, 1, r + 1)()
                split_lo(2 * u0 + 7)
                gx_rest(n, 1)()
                for f in (2, 3):
                    unit(u0 + f, add_to_residual(u0 + f, f, r + f), second=[gx_rest(n, f)])
                with dve.Fori(1, 4) as i:
                    for s in range(4):
                        unit(u0 + s, add_to_residual(u0 + s, s, r + s, 4 * i, 4 * i, 4 * i), 4 * i,
                             second=[gx_rest(n, s, 4 * i)])

            out_projection(U_OUT0, N_FFN0, 0, second=[lo_part(KT - 1, ps_aux[:, 0:SEQ])])

            def hidden_in(layer):
                c0 = (COPIES_FF0, COPIES_FF1)[layer]
                m0 = (MID_FF0, MID_FF1)[layer]
                k0 = layer * FF_CHUNKS * KT

                def run(u, f, k, o=0, of=0, ok=0, chunk=0):
                    c, k_in = c0 + k - k0, k

                    def evac():
                        sum_product(u, c, o, ok)
                        dve.scalar_tensor_tensor(relu[:], summed[:], 0.0, rstd[:], ALU.max, ALU.mult
                                                 ).then_inc(relu_done, 1)
                        dve.wait_ge(relu_done, k_in + 1 + ok)
                        dve.wait_ge(mid_ready, m0 + k - k0 + ok)
                        dve.tensor_tensor(square[:], relu[:], relu[:], ALU.mult).then_inc(squared, 1)

                    def lo_hidden():
                        dve.wait_ge(mid_hi, m0 + k - k0 + 1 + ok)
                        dve.tensor_tensor(mid[:, f + of, SEQ:], square[:], mid[:, f + of, 0:SEQ].bitcast(F32),
                                          ALU.subtract).then_inc(mid_ready, 1)

                    if f == 0 and isinstance(o, int) and u in (U_FF0, U_FF1):
                        first_unit(u, (N_FFN0, N_FFN1)[layer], evac, second=[lo_hidden])
                    else:
                        unit(u, evac, o, second=[lo_hidden])
                return run

            def output_in(r0, layer):
                def run(u, f, k, o=0, of=0, ok=0, chunk=0):
                    r = r0 + k - layer * FF_CHUNKS * KT
                    unit(u, add_to_residual(u, f, r, o, of, ok), o)
                return run

            def last_output_in(r0, layer, n):
                def run(u, f, k, o=0, of=0, ok=0, chunk=0):
                    r = r0 + k - layer * FF_CHUNKS * KT
                    unit(u, add_to_residual(u, f, r, o, of, ok), o, second=[gx_rest(n, f, of)],
                         split=u + 2 < UNITS)
                return run

            dve.wait_ge(proj_ready, U_OUT0)
            feed_forward(dve, 0, U_FF0, hidden_in(0), output_in(KT, 0), last_output_in(KT, 0, N_MIX1),
                         clear_sum)

            first_unit(U_QKV1, N_MIX1, projected(U_QKV1, COPIES_QKV1, q0, SCALE))
            unit(U_QKV1 + 1, projected(U_QKV1 + 1, COPIES_QKV1 + 1, k0))
            dve.wait_ge(bias_second, 16 * QT)
            dve.wait_ge(lam_steps, 4)

            def combine(h, oh=0):
                def step():
                    n = A_HEADS + 4 * h
                    dve.wait_ge(exp_done, QT * A_HEADS + 4 * (h + 1) + 4 * oh)
                    dve.wait_ge(attn_ready, QT * (A_HEADS + h + oh))
                    dve.reciprocal(row_inv[:], row_sum[:]).then_inc(soft_steps, 1)
                    dve.wait_ge(soft_steps, n + 1 + 4 * oh)
                    dve.tensor_scalar(lam_inv[:], row_inv[:, 1, :], neg_lam[:], None, ALU.mult
                                      ).then_inc(soft_steps, 1)
                    for t in range(QT):
                        dve.tensor_scalar(part0[:, t, :], probs[:, 0, t, :], row_inv[:, 0, t:t + 1], None, ALU.mult
                                          ).then_inc(soft_steps, 1)
                    dve.wait_ge(soft_steps, n + 4 + 4 * oh)
                    dve.wait_ge(pt_ready, A_HEADS + h + oh)
                    for t in range(QT):
                        dve.scalar_tensor_tensor(attn[:, t, :], probs[:, 1, t, :], lam_inv[:, t:t + 1],
                                                 part0[:, t, :], ALU.mult, ALU.add).then_inc(attn_ready, 1)
                return step

            def head_norm(h, oh=0):
                def step():
                    dve.wait_ge(osq_done, QT * (h + 1 + oh))
                    dve.tensor_scalar(o_mean[:], o_sum[:], 1.0 / (2 * P), EPS, ALU.mult, ALU.add
                                      ).then_inc(omean_ready, 1)
                    dve.wait_ge(oinv_ready, h + 1 + oh)
                    dve.wait_ge(ot_ready, h + oh)
                    for t in range(QT):
                        dve.tensor_scalar(o_norm[:, t, :], ps_o[:, t * SEQ:(t + 1) * SEQ], o_inv[:, t:t + 1], None,
                                          ALU.mult).then_inc(onorm_ready, 1)
                return step

            def lo_att1(h, oh=0):
                def step():
                    dve.wait_ge(mid_hi, MID_ATT1 + 2 * (h + 1) + 2 * oh)
                    for j in range(2):
                        t = 2 * h + j + 2 * oh
                        dve.scalar_tensor_tensor(mid[:, t, SEQ:], ps_aux[:, j * SEQ:(j + 1) * SEQ],
                                                 sub_gain[:, j:j + 1], mid[:, t, 0:SEQ].bitcast(F32),
                                                 ALU.mult, ALU.subtract).then_inc(mid_ready, 1)
                return step

            def head1(h, oh=0):
                u, c = U_QKV1 + 2 + 6 * h, COPIES_QKV1 + 2 + 6 * h
                o, s, e = 6 * oh, A_HEADS + 2 * h, QT * A_HEADS + 4 * h

                def proj(k, dst, scale=1.0):
                    return projected(u + k, c + k, dst, scale, o, o)

                unit(u, proj(0, q_t[:, 1, ::-1], SCALE), o, first=[score_rows(0, s, e, h, 2 * oh, 4 * oh, oh)])
                unit(u + 1, proj(1, k_t[:, 1, :]), o)
                unit(u + 2, proj(2, v_t[:, 0, :]), o,
                     first=[score_rows(1, s + 1, e, h, 2 * oh, 4 * oh, oh), combine(h, oh)])
                unit(u + 3, proj(3, v_t[:, 1, :]), o)
                if h < C_HEADS - 1:
                    unit(u + 4, proj(4, q0, SCALE), o)
                    unit(u + 5, proj(5, k0), o, before=[head_norm(h, oh)], second=[lo_att1(h, oh)])

            head1(0)
            with dve.Fori(0, 3) as i:
                for h in (1, 2):
                    head1(h, 2 * i)
            head1(7)
            out_projection(U_OUT1, N_FFN1, KT * (1 + FF_CHUNKS), first=[head_norm(C_HEADS - 1)],
                           second=[lo_att1(C_HEADS - 1)])
            dve.wait_ge(proj_ready, U_OUT0 + 6 * C_HEADS)
            feed_forward(dve, 1, U_FF1, hidden_in(1), output_in(KT * (2 + FF_CHUNKS), 1),
                         last_output_in(KT * (2 + FF_CHUNKS), 1, N_FINAL), clear_sum)

            token_stats(N_FINAL)
            token_rstd(N_FINAL)
            for g in range(3):
                for f in range(4 * g, 4 * g + 4):
                    ins = dve.tensor_tensor(y_out[:, f, :], y_out[:, f, :], rstd[:], ALU.mult)
                ins.then_inc(y_ready, 1)

        @block.tensor
        def _(pe):
            def half(n, u, kts, operand, o=0, hooks=None, whole=None, tile_wait=None):
                hooks = hooks or {}
                pe.wait_ge(lo_ready, n + 1 + 2 * o)
                for j, kt in enumerate(kts):
                    for step in hooks.get(j, ()):
                        step()
                    if tile_wait is not None:
                        ready, base, first = tile_wait
                        if kt == 0 or kt >= first:
                            pe.wait_ge(ready, base + (kt + 1 if kt else first))
                    cols = slice(j * P, (j + 1) * P)

                    def hi():
                        return pe.matmul(acc_of(u)[:], w_hi[:, n % RING, cols], operand[:, kt, :], start=kt == 0,
                                         stop=kt == KT - 1)

                    def lo():
                        return pe.matmul(acc_of(u)[:, SEQ:], w_lo[:, n % RING, cols], operand[:, kt, 0:SEQ],
                                         start=False, stop=False)

                    if kt == KT - 1:
                        lo()
                        ins = hi()
                    else:
                        hi()
                        ins = lo()
                ins.then_inc(w_used, 1)
                for step in hooks.get(KT // 2, ()):
                    step()

            FIRST, SECOND = range(0, KT // 2), range(KT // 2, KT)

            def unit(u, operand, o=0, hooks=({}, {}), tile_wait=None):
                if u >= 3:
                    pe.wait_ge(acc_free, u - 1 + o)
                half(2 * u, u, FIRST, operand, o, hooks[0], tile_wait=tile_wait)
                half(2 * u + 1, u, SECOND, operand, o, hooks[1], tile_wait=tile_wait)

            def stat_sum(n):
                def step():
                    if n == N_MIX0:
                        pe.wait_ge(x0_summed, int(math.log2(KT)))
                    else:
                        pe.wait_ge(sum_steps, SUMS_BEFORE[n + 1])
                    for t in range(QT):
                        ins = pe.matmul(ps_aux[:, t:t + 1], sum_sq[:, t * P:(t + 1) * P], ones[:, 0:1],
                                        start=True, stop=True)
                    ins.then_inc(stat_ready, 1)
                return step

            def stat_spread(n):
                def step():
                    pe.wait_ge(diag_ready, QT * (n + 1))
                    for t in range(QT):
                        ins = pe.matmul(ps_aux[:, t * P:(t + 1) * P], ones[:], diag[:, t, :], start=True, stop=True)
                    ins.then_inc(bcast_ready, 1)
                return step

            def scores(m, s, proj, read, os=0, op=0, orr=0):
                def step():
                    pe.wait_ge(proj_ready, proj + op)
                    pe.wait_ge(scores_read, read + orr)
                    for t in range(QT):
                        ins = pe.matmul(ps_scores[m][:, t, :], q_t[:, m, t * P:(t + 1) * P], k_t[:, m, :],
                                        start=True, stop=True)
                    ins.then_inc(scores_ready, 1)
                return step

            def turn_v(n, proj, tiles, oh=0, op=0):
                def step():
                    pe.wait_ge(proj_ready, proj + op)
                    pe.wait_ge(v_copied, n + oh)
                    for kt in range(QT):
                        for j in range(tiles):
                            ins = pe.transpose(ps_v[:, kt, j * P:(j + 1) * P], v_t[:, j, kt * P:(kt + 1) * P], ident[:])
                    ins.then_inc(vt_ready, 1)
                return step

            def turn_attn(n, oh=0):
                def step():
                    pe.wait_ge(attn_ready, QT * (n + 1) + QT * oh)
                    pe.wait_ge(pt_copied, n + oh)
                    for kt in range(QT):
                        for t in range(QT):
                            ins = pe.transpose(ps_attn_t[:, kt, t * P:(t + 1) * P], attn[:, t, kt * P:(kt + 1) * P],
                                               ident[:])
                    ins.then_inc(pt_ready, 1)
                return step

            def attend0(h, oh=0):
                def step():
                    pe.wait_ge(v_copied, h + 1 + oh)
                    pe.wait_ge(pt_copied, h + 1 + oh)
                    pe.wait_ge(mid_ready, h + oh)
                    for kt in range(QT):
                        ins = pe.matmul(ps_o[:, 0:SEQ], v_tok[:, kt, 0:P], attn_t[:, kt, :], start=kt == 0,
                                        stop=kt == QT - 1)
                    ins.then_inc(o_ready, 1)
                return step

            def mix_channels(g):
                def step():
                    pe.wait_ge(proj_ready, 3 * A_HEADS + g + 1)
                    pe.wait_ge(mix_copied, g)
                    for t in range(QT):
                        ins = pe.matmul(ps_scores[1][:, t, :], u_t[:, t * P:(t + 1) * P],
                                        ch_map[:, g, :, :].rearrange("p r e -> p (r e)"), start=True, stop=True)
                    ins.then_inc(mix1_ready, 1)
                return step

            def mix_positions(g):
                def step():
                    pe.wait_ge(mix_copied, g + 1)
                    pe.wait_ge(mid_ready, A_HEADS + g)
                    for t in range(QT):
                        for r in range(2):
                            ins = pe.matmul(ps_aux[:, 0:SEQ], mixed[:, t, r * P:(r + 1) * P], pos_dft[:, t, r, :],
                                            start=t == r == 0, stop=t == r == 1)
                    ins.then_inc(mix2_ready, 1)
                return step

            pe.wait_ge(ones_ready, 1)
            pe.wait_ge(tab_landed, 16 * 3)
            pe.matmul(ps_scores[0][0:HEADS, :, :].rearrange("p t k -> p (t k)"), tab[:], one_hot, start=True,
                      stop=True).then_inc(line_ready, 1)

            def group_maps():
                pe.wait_ge(dft_landed, 16 * 3)
                for r, bank in enumerate((ps_o[:], ps_attn_t[:].rearrange("p t k -> p (t k)"))):
                    for g in range(GROUPS):
                        ins = pe.matmul(bank[:, g * P:(g + 1) * P], ch_dft[:, r, :], wf[:, g, :], start=True, stop=True)
                ins.then_inc(map_ready, 1)
                pe.wait_ge(lam_steps, 1)
                pe.matmul(ps_v[:, 0, 0:2], ones[:], lam_prod[:], start=True, stop=True).then_inc(lam_sum_ready, 1)
                pe.wait_ge(small_landed, 16 * 3)

            unit(0, gx, tile_wait=(gx_ready, 0, 1))
            unit(1, gx, hooks=({}, {4: [stat_sum(N_MIX0)]}))

            def first_scores():
                pe.wait_ge(line_copied, 1)
                scores(0, 0, 2, 0)()

            def first_turn():
                pe.wait_ge(map_copied, 1)
                pe.wait_ge(lam_exp_ready, 1)
                turn_v(0, 3, 1)()
                turn_attn(0)()

            def head0(h, oh=0):
                u, o = 2 + 3 * h, 3 * oh
                if h == 0:
                    unit(u, gx, hooks=({4: [stat_spread(N_MIX0)]}, {4: [group_maps], 8: [first_scores]}))
                else:
                    unit(u, gx, o, hooks=({8: [scores(0, h, u, h, oh, o, oh)]}, {}))
                unit(u + 1, gx, o, hooks=({}, {4: [turn_v(h, u + 1, 1, oh, o), turn_attn(h, oh)] if h else [first_turn]}))
                if h < A_HEADS - 1:
                    unit(u + 2, gx, o, hooks=({8: [attend0(h, oh)]}, {}))
                else:
                    unit(u + 2, gx, o, hooks=({8: [attend0(h, oh), mix_channels(0)]}, {8: [mix_positions(0)]}))

            head0(0)
            with pe.Fori(0, 2) as i:
                for h in range(1, 5):
                    head0(h, 4 * i)
            for h in range(9, A_HEADS):
                head0(h)
            for g in (1, 2):
                unit(U_OUT0 - 3 + g, gx, hooks=({8: [mix_channels(g)]}, {8: [mix_positions(g)]}))

            def out_projection(u0, mid0, hooks):
                pe.wait_ge(acc_free, u0 - 1)
                half(2 * u0, u0, FIRST, mid, hooks=hooks[0], tile_wait=(mid_ready, mid0, KT // 2))
                pe.wait_ge(acc_free, u0)
                half(2 * u0 + 1, u0 + 1, FIRST, mid, hooks=hooks[1])
                half(2 * u0 + 2, u0, SECOND, mid, hooks=hooks[2], tile_wait=(mid_ready, mid0, KT // 2))
                half(2 * u0 + 3, u0 + 1, SECOND, mid)
                for f in (2, 3):
                    unit_in_pairs(u0 + f)
                with pe.Fori(1, 4) as i:
                    for s in range(4):
                        unit(u0 + s, mid, 4 * i)

            def unit_in_pairs(u):
                unit(u, mid)

            out_projection(U_OUT0, MID_ATT0, ({8: [mix_channels(3)]}, {8: [mix_positions(3)]}, {}))

            def hidden(u, f, k, o=0, of=0, ok=0, chunk=0):
                if u in (U_FF0, U_FF1) and isinstance(o, int):
                    n = N_FFN0 if u == U_FF0 else N_FFN1
                    unit(u, gx, tile_wait=(gx_ready, GX_BEFORE[n], KT // 2), hooks=({}, {4: [stat_sum(n)]}))
                elif u in (U_FF0 + 1, U_FF1 + 1) and isinstance(o, int):
                    n = N_FFN0 if u == U_FF0 + 1 else N_FFN1
                    unit(u, gx, hooks=({4: [stat_spread(n)]}, {}))
                else:
                    unit(u, gx, o)

            def output(u, f, k, o=0, of=0, ok=0, chunk=0):
                layer = k // (FF_CHUNKS * KT)
                base = (MID_FF0, MID_FF1)[layer] + (k - f) - layer * FF_CHUNKS * KT
                unit(u, mid, o, tile_wait=(mid_ready, base + chunk, KT // 2) if f == 0 else None)

            feed_forward(pe, 0, U_FF0, hidden, output, output)

            unit(U_QKV1, gx, tile_wait=(gx_ready, GX_BEFORE[N_MIX1], KT // 2), hooks=({}, {4: [stat_sum(N_MIX1)]}))
            unit(U_QKV1 + 1, gx, hooks=({4: [stat_spread(N_MIX1)]}, {}))

            def attend1(h, oh=0):
                def step():
                    n = A_HEADS + h
                    pe.wait_ge(v_copied, n + 1 + oh)
                    pe.wait_ge(pt_copied, n + 1 + oh)
                    for t in range(QT):
                        for kt in range(QT):
                            ins = pe.matmul(ps_o[:, t * SEQ:(t + 1) * SEQ], attn_t[:, kt, t * P:(t + 1) * P],
                                            v_tok[:, kt, :], start=kt == 0, stop=kt == QT - 1)
                    ins.then_inc(o_ready, 1)
                return step

            def turn_output(h, oh=0):
                def step():
                    pe.wait_ge(onorm_ready, QT * (h + 1) + QT * oh)
                    pe.wait_ge(mid_ready, MID_ATT1 + 2 * h + 2 * oh)
                    for j in range(2):
                        for t in range(QT):
                            ins = pe.transpose(ps_aux[:, j * SEQ + t * P:j * SEQ + (t + 1) * P],
                                               o_norm[:, t, j * P:(j + 1) * P], ident[:])
                    ins.then_inc(ot_ready, 1)
                return step

            def head1(h, oh=0):
                u, o, n = U_QKV1 + 2 + 6 * h, 6 * oh, A_HEADS + h
                p, s, read = U_OUT0 + 2 + 6 * h, A_HEADS + 2 * h, A_HEADS + 2 * h
                unit(u, gx, o, hooks=({8: [scores(0, s, p, read, 2 * oh, o, 2 * oh)]}, {}))
                unit(u + 1, gx, o)
                unit(u + 2, gx, o, hooks=({8: [scores(1, s + 1, p + 2, read, 2 * oh, o, 2 * oh)]}, {}))
                unit(u + 3, gx, o, hooks=({}, {4: [turn_attn(n, oh)]}))
                if h < C_HEADS - 1:
                    unit(u + 4, gx, o, hooks=({8: [turn_v(n, p + 4, 2, oh, o)]}, {8: [attend1(h, oh)]}))
                    unit(u + 5, gx, o, hooks=({}, {8: [turn_output(h, oh)]}))

            head1(0)
            with pe.Fori(0, 3) as i:
                for h in (1, 2):
                    head1(h, 2 * i)
            head1(7)
            last = C_HEADS - 1
            out_projection(U_OUT1, MID_ATT1,
                           ({8: [turn_v(HEADS - 1, U_OUT0 + 6 * C_HEADS, 2)]}, {4: [attend1(last)]},
                            {3: [turn_output(last)]}))
            feed_forward(pe, 1, U_FF1, hidden, output, output)
            stat_sum(N_FINAL)()
            stat_spread(N_FINAL)()


GX_BEFORE = {n: KT * n for n in range(N_FINAL)}


def feed_forward(eng, layer, u0, hidden, output, last_output, before_last=None):
    k0 = layer * FF_CHUNKS * KT

    def run(what, u, k, c_off, i_from, i_to):
        with eng.Fori(i_from, i_to) as i:
            for s in range(4):
                what(u + s, s, k + s, 2 * KT * c_off + 4 * i, 4 * i, KT * c_off + 4 * i, KT * c_off)

    for s in range(4):
        hidden(u0 + s, s, k0 + s)
    run(hidden, u0, k0, 0, 1, KT // 4)
    run(output, u0 + KT, k0, 0, 0, KT // 4)
    with eng.Fori(0, FF_CHUNKS - 2) as c:
        run(hidden, u0 + 2 * KT, k0 + KT, c, 0, KT // 4)
        run(output, u0 + 3 * KT, k0 + KT, c, 0, KT // 4)
    u, k = u0 + 2 * KT * (FF_CHUNKS - 1), k0 + KT * (FF_CHUNKS - 1)
    run(hidden, u, k, 0, 0, KT // 4)
    if before_last is not None:
        before_last()
    tail = 4 if layer == 1 else 0
    run(last_output, u + KT, k, 0, 0, (KT - tail) // 4)
    for s in range(KT - tail, KT):
        last_output(u + KT + s, s, k + s)


def stream_units(w_in, w_out0, ff1, ff2, w_qkv, w_out1):
    def tiles(w):
        return w.reshape(w.shape[0] // P, P, w.shape[1] // P, P).transpose(2, 1, 0, 3)

    def by_halves(w):
        t = tiles(w)
        a, b = t[0], t[1]
        h = KT // 2
        pair = np.stack([np.concatenate([a[:, :h], b[:, :h]], axis=1), np.concatenate([a[:, h:], b[:, h:]], axis=1)])
        return np.concatenate([pair, t[2:]])

    def mlp(w1, w2):
        up, down = tiles(w1), tiles(w2)
        parts = []
        for c in range(FF_CHUNKS):
            parts += [up[c * KT:(c + 1) * KT], down[:, :, c * KT:(c + 1) * KT]]
        return parts

    t = tiles(w_in)
    order0 = [x for h in range(A_HEADS) for x in (h, A_HEADS + h, 2 * A_HEADS + h)]
    order0 += [3 * A_HEADS + g for g in range(GROUPS)]
    q = tiles(w_qkv)
    n = 2 * C_HEADS
    order1 = [x for h in range(C_HEADS)
              for x in (2 * h, n + 2 * h, 2 * h + 1, n + 2 * h + 1, 2 * n + 2 * h, 2 * n + 2 * h + 1)]
    parts = [t[order0], by_halves(w_out0), *mlp(ff1[0], ff2[0]), q[order1], by_halves(w_out1), *mlp(ff1[1], ff2[1])]
    return np.concatenate(parts).reshape(UNITS, P, KT * P)


def shape_constants():
    d = np.arange(-(SEQ - 1), SEQ)
    n = np.abs(d)
    max_exact = BUCKETS // 4
    large = max_exact + (np.log(np.maximum(n, 1).astype(np.float32) / np.float32(max_exact)).astype(np.float32)
                         / np.float32(math.log(1024 / max_exact)) * np.float32(BUCKETS // 2 - max_exact)
                         ).astype(np.int32)
    bucket = np.where(d > 0, BUCKETS // 2, 0) + np.where(n < max_exact, n, np.minimum(large, BUCKETS // 2 - 1))
    onehot = np.zeros((BUCKETS + 1, LINE), np.float32)
    onehot[bucket, np.arange(d.size)] = 1.0
    reach = sum(((n % dil == 0) & (n <= window // 2)).astype(int) for window, dil in ((128, 1), (512, 4), (2048, 16)))
    onehot[BUCKETS, :d.size] = np.where(reach > 0, np.log(np.maximum(reach, 1)), -1e30)
    a_head_row = np.zeros((1, HEADS), np.float32)
    a_head_row[0, :A_HEADS] = 1.0
    c = np.arange(P)
    angle = 2 * np.pi * (np.outer(c, c) % P) / P
    channel = np.stack([np.cos(angle), np.sin(angle)], axis=1).astype(np.float32)
    s = np.arange(SEQ)
    angle = (2 * np.pi * (np.outer(s, s) % SEQ) / SEQ).reshape(QT, P, SEQ).transpose(1, 0, 2)
    position = (np.stack([np.cos(angle), -np.sin(angle)], axis=2) / math.sqrt(SEQ * P)).astype(np.float32)
    return onehot, a_head_row, channel, position, np.eye(P, dtype=np.float32)


def kernel(x, norm_mix_g, norm_ffn_g, norm_final_g, rel_bias_table, w_in_even, w_fnet, w_out_even, w_qkv_odd,
           lambda_q1, lambda_k1, lambda_q2, lambda_k2, subln_g, w_out_odd, w_ff1, w_ff2):
    import concourse.bacc as bacc
    from concourse.bass_utils import run_bass_kernel_spmd

    onehot, a_head_row, channel, position, identity = shape_constants()
    gains = np.stack([norm_mix_g[0], norm_ffn_g[0], norm_mix_g[1], norm_ffn_g[1], norm_final_g])
    arrays = {
        "xT": np.ascontiguousarray(np.asarray(x)[0].T),
        "weights": stream_units(*(np.asarray(a) for a in (w_in_even[0], w_out_even[0], w_ff1, w_ff2, w_qkv_odd[0],
                                                          w_out_odd[0]))),
        "gains": np.ascontiguousarray(gains.reshape(5, KT, P).transpose(2, 0, 1)),
        "subln": np.ascontiguousarray(np.asarray(subln_g)[0].reshape(2, P).T),
        "lambdas": np.ascontiguousarray(np.concatenate([lambda_q1, lambda_k1, lambda_q2, lambda_k2]).T),
        "table": np.ascontiguousarray(rel_bias_table),
        "w_fnet": np.ascontiguousarray(np.asarray(w_fnet)[0]),
        "onehot": onehot, "a_head_row": a_head_row, "channel_dft": channel, "position_dft": position,
        "identity": identity,
    }
    nc = bacc.Bacc("TRN2", target_bir_lowering=False, num_devices=1)
    aps = {name: nc.dram_tensor(f"{name}_dram", a.shape, mybir.dt.from_np(a.dtype), kind="ExternalInput").ap()
           for name, a in arrays.items()}
    out = nc.dram_tensor("out_dram", (D, SEQ), F32, kind="ExternalOutput").ap()
    trunk(nc, outT=out, **aps)
    result = run_bass_kernel_spmd(nc, [{f"{name}_dram": a for name, a in arrays.items()}], core_ids=[0])
    return np.ascontiguousarray(result.results[0]["out_dram"].T)[None]
```

```python
from contextlib import ExitStack
import math

import numpy as np
import concourse.bass as bass
from concourse import mybir

F32 = mybir.dt.float32
F32R = mybir.dt.float32r
ALU = mybir.AluOpType
ACT = mybir.ActivationFunctionType
AX_X = mybir.AxisListType.X

P = 128
D = 2048
SEQ = 256
KT = D // P
QT = SEQ // P
A_HEADS, GROUPS, C_HEADS = 12, 4, 8
HEADS = A_HEADS + C_HEADS
BUCKETS = 32
FF_CHUNKS = 4
EPS = 1e-6
SCALE = 1.0 / math.sqrt(P)
LAMBDA_INIT = 0.8 - 0.6 * math.exp(-0.3 * 1)
LINE = 2 * SEQ

HALF = KT // 2 * P
RAW_SLOTS = 4
RING = 4

U_QKV0 = 0
U_OUT0 = U_QKV0 + 3 * A_HEADS + GROUPS
U_FF0 = U_OUT0 + KT
U_QKV1 = U_FF0 + 2 * KT * FF_CHUNKS
U_OUT1 = U_QKV1 + 6 * C_HEADS
U_FF1 = U_OUT1 + KT
UNITS = U_FF1 + 2 * KT * FF_CHUNKS

MID_ATT0, MID_FF0 = 0, KT
MID_ATT1 = MID_FF0 + KT * FF_CHUNKS
MID_FF1 = MID_ATT1 + KT

COPIES_QKV0, COPIES_FF0 = 0, U_OUT0
COPIES_QKV1 = COPIES_FF0 + KT * FF_CHUNKS
COPIES_FF1 = COPIES_QKV1 + 6 * C_HEADS

N_MIX0, N_FFN0, N_MIX1, N_FFN1, N_FINAL = range(5)
SUMS_BEFORE = {n: (KT + 1) * (n - 1) for n in range(1, 6)}
SQUARES_BEFORE = {n: KT * (n - 1) for n in range(1, 5)}
Y_GROUPS, Y_LAST = ((0, 2), (2, 5), (5, 9), (9, 13)), (13, 16)
BIAS_FIRST = A_HEADS - KT // QT


def trunk(nc, xT, weights, gains, subln, lambdas, table, w_fnet, onehot, a_head_row, channel_dft,
          position_dft, identity, outT):
    ctx = ExitStack()
    with ctx:
        def sb(name, shape, dt=F32):
            return ctx.enter_context(nc.sbuf_tensor(name, shape, dt))

        def pb(name, shape):
            return ctx.enter_context(nc.psum_tensor(name, shape, F32))

        def sem(name):
            return ctx.enter_context(nc.semaphore(name))

        x = sb("x", [P, KT, SEQ])
        gx = sb("gx", [P, KT, 2 * SEQ], F32R)
        mid = sb("mid", [P, KT, 2 * SEQ], F32R)
        raw = sb("raw", [P, RAW_SLOTS, 2 * HALF])
        w_hi = sb("w_hi", [P, RING, HALF], F32R)
        w_lo = sb("w_lo", [P, RING, HALF], F32R)
        bias = sb("bias", [P, A_HEADS, QT, SEQ])
        y_out = bias[:].rearrange("p h t k -> p (h t k)")[:, 0:KT * SEQ].rearrange(
            "p (f t) -> p f t", f=KT)
        x0_sq = bias[:, BIAS_FIRST:A_HEADS, :, :].rearrange("p h t k -> p (h t) k")
        line = bias[0:HEADS, 0, :, :].rearrange("h t k -> h (t k)")
        one_hot = bias[0:BUCKETS + 1, 1, :, :].rearrange("b t k -> b (t k)")
        gain = sb("gain", [P, 5, KT])
        sub_gain = sb("sub_gain", [P, 2])
        sub_gain_in = sb("sub_gain_in", [P, 2])
        lam_in = sb("lam_in", [P, 4])
        lam_prod = sb("lam_prod", [P, 2])
        lam_exp = sb("lam_exp", [P, 2])
        lam_diff = sb("lam_diff", [P, 1])
        neg_lam = sb("neg_lam", [P, 1])
        tab = sb("tab", [BUCKETS + 1, HEADS])
        ch_dft = sb("ch_dft", [P, 2, P])
        pos_dft = sb("pos_dft", [P, QT, 2, SEQ])
        ch_map = sb("ch_map", [P, GROUPS, 2, P])
        mixed = sb("mixed", [P, QT, 2 * P])
        ident = sb("ident", [P, P])
        ones = sb("ones", [P, P])
        minus_half = sb("minus_half", [P, 2])
        copied = sb("copied", [P, SEQ])
        summed = sb("summed", [P, SEQ])
        relu = sb("relu", [P, SEQ])
        square = sb("square", [P, SEQ])
        x_sq, proj_full = relu, relu
        sum_sq = square
        rstd = sb("rstd", [P, SEQ])
        mean_sq = sb("mean_sq", [P, QT])
        rstd_col = sb("rstd_col", [P, QT])
        q_t = sb("q_t", [P, 2, SEQ], F32R)
        k_t = sb("k_t", [P, 2, SEQ], F32R)
        v_t = sb("v_t", [P, 2, SEQ])
        u_t = v_t[:, 1, :]
        v_tok = sb("v_tok", [P, 2, QT, 2 * P], F32R)
        logits = sb("logits", [P, 2, QT, SEQ])
        probs = logits
        wf = logits[:, 1, :, :].rearrange("p t (g e) -> p (t g) e", e=P)
        row_max = sb("row_max", [P, 2, QT])
        neg_max = sb("neg_max", [P, 2, QT])
        row_sum = sb("row_sum", [P, 2, QT])
        row_inv = sb("row_inv", [P, 2, QT])
        lam_inv = sb("lam_inv", [P, QT])
        part0, o_norm = pos_dft[:, 0, :, :], pos_dft[:, 1, :, :]
        attn = sb("attn", [P, QT, SEQ])
        diag = attn[:, :, 0:P]
        attn_t = sb("attn_t", [P, 2, QT, SEQ], F32R)
        o_sq = mixed
        o_sum = sb("o_sum", [P, QT])
        o_mean = sb("o_mean", [P, QT])
        o_inv = sb("o_inv", [P, QT])

        acc = [pb(f"acc{i}", [P, 2 * SEQ]) for i in range(2)]
        ps_scores = [pb(f"ps_scores{i}", [P, QT, SEQ]) for i in range(2)]
        ps_attn_t = pb("ps_attn_t", [P, QT, SEQ])
        ps_v = pb("ps_v", [P, QT, 2 * P])
        ps_o = pb("ps_o", [P, 2 * SEQ])
        ps_aux = pb("ps_aux", [P, 2 * SEQ])

        bias_line = nc.dram_tensor("bias_line", (HEADS, LINE), F32, kind="Internal").ap()

        raw_landed = [sem(f"raw_landed{i}") for i in range(RAW_SLOTS)]
        first_half_landed = sem("first_half_landed")
        hi_ready, lo_ready = sem("hi_ready"), sem("lo_ready")
        w_used = sem("w_used")
        acc_free = sem("acc_free")
        acc_half = sem("acc_half")
        copy_ready = sem("copy_ready")
        proj_ready = sem("proj_ready")
        relu_done, squared = sem("relu_done"), sem("squared")
        mid_hi, mid_ready = sem("mid_hi"), sem("mid_ready")
        gx_hi, gx_ready = sem("gx_hi"), sem("gx_ready")
        xsq_done, sum_steps = sem("xsq_done"), sem("sum_steps")
        stat_ready, mean_ready = sem("stat_ready"), sem("mean_ready")
        inv_ready, diag_ready = sem("inv_ready"), sem("diag_ready")
        bcast_ready, rstd_ready = sem("bcast_ready"), sem("rstd_ready")
        scores_ready, scores_read = sem("scores_ready"), sem("scores_read")
        max_done, neg_ready, exp_done = sem("max_done"), sem("neg_ready"), sem("exp_done")
        soft_steps, attn_ready = sem("soft_steps"), sem("attn_ready")
        qk_hi, qk_ready = sem("qk_hi"), sem("qk_ready")
        v_split, pt_split = sem("v_split"), sem("pt_split")
        vt_ready, pt_ready = sem("vt_ready"), sem("pt_ready")
        v_copied, pt_copied, o_ready = sem("v_copied"), sem("pt_copied"), sem("o_ready")
        osq_done, omean_ready = sem("osq_done"), sem("omean_ready")
        oinv_ready, onorm_ready, ot_ready = sem("oinv_ready"), sem("onorm_ready"), sem("ot_ready")
        mix1_ready, mix_copied, mix2_ready = sem("mix1_ready"), sem("mix_copied"), sem("mix2_ready")
        x_landed = [sem(f"x_landed{i}") for i in range(4)]
        small_landed, tab_landed, dft_landed = sem("small_landed"), sem("tab_landed"), sem("dft_landed")
        gain_landed, ones_ready = sem("gain_landed"), sem("ones_ready")
        map_ready, map_copied = sem("map_ready"), sem("map_copied")
        line_ready, line_copied, line_stored = sem("line_ready"), sem("line_copied"), sem("line_stored")
        bias_first, bias_rest, bias_second = sem("bias_first"), sem("bias_rest"), sem("bias_second")
        x0_squared, x0_summed = sem("x0_squared"), sem("x0_summed")
        lam_steps, lam_sum_ready, lam_exp_ready = sem("lam_steps"), sem("lam_sum_ready"), sem("lam_exp_ready")
        y_last_ready, y_ready, y_stored = sem("y_last_ready"), sem("y_ready"), sem("y_stored")

        def acc_of(u):
            return ps_scores[1][:].rearrange("p t k -> p (t k)") if u == 2 else acc[u % 2][:]

        def load_bias(eng, landed, line_head, first, last):
            for t in range(QT):
                src = bass.AP(bias_line.tensor, line_head * LINE + P * t, [[1, P], [LINE, last - first], [1, SEQ]])
                eng.dma_start(bias[:, first:last, t, :], src).then_inc(landed, 16)

        def scale_rows(eng, lo, hi):
            return eng.tensor_tensor(y_out[:, lo:hi, :], y_out[:, lo:hi, :],
                                     rstd[:].unsqueeze(1).to_broadcast([P, hi - lo, SEQ]), ALU.mult)

        block = ctx.enter_context(nc.Block())

        @block.sync
        def _(sp):
            def load(u, o=0, free=True):
                slot = u % RAW_SLOTS
                if free:
                    sp.wait_ge(lo_ready, 2 * (u - RAW_SLOTS + 1) + 2 * o)
                sp.dma_start(raw[:, slot, :], weights[u + o]).then_inc(raw_landed[slot], 16)

            def load_x(g):
                sp.dma_start(x[:, 4 * g:4 * g + 4, :], xT.rearrange("(f p) t -> p f t", p=P)[:, 4 * g:4 * g + 4, :]
                             ).then_inc(x_landed[g], 16)

            sp.dma_start(raw[:, 0, 0:HALF], weights[0, :, 0:HALF]).then_inc(first_half_landed, 16)
            sp.dma_start(gain[:], gains).then_inc(gain_landed, 16)
            load_x(0)
            sp.dma_start(raw[:, 0, HALF:], weights[0, :, HALF:]).then_inc(raw_landed[0], 16)
            for g in range(1, 4):
                load_x(g)
            load(1, free=False)
            sp.wait_ge(line_copied, 1)
            sp.dma_start(bias_line, line).then_inc(line_stored, 16)
            load(2, free=False)
            sp.wait_ge(line_stored, 16)
            load_bias(sp, bias_first, 0, 0, BIAS_FIRST)
            load(3, free=False)
            load(4)
            load(5)
            sp.wait_ge(stat_ready, 1)
            load_bias(sp, bias_rest, BIAS_FIRST, BIAS_FIRST, A_HEADS)
            load(6)
            load(7)
            with sp.Fori(1, UNITS // RAW_SLOTS - 1) as i:
                for s in range(RAW_SLOTS):
                    load(RAW_SLOTS + s, RAW_SLOTS * i)
            for ready, count, (lo, hi) in ((y_ready, 1, Y_GROUPS[0]), (y_ready, 2, Y_GROUPS[1]),
                                           (y_ready, 3, Y_GROUPS[2]), (y_last_ready, 1, Y_LAST),
                                           (y_ready, 4, Y_GROUPS[3])):
                sp.wait_ge(ready, count)
                sp.dma_start(outT.rearrange("(f p) t -> p f t", p=P)[:, lo:hi, :],
                             y_out[:, lo:hi, :]).then_inc(y_stored, 16)
            sp.wait_ge(y_stored, 16 * (len(Y_GROUPS) + 1))

        @block.gpsimd
        def _(pool):
            pool.memset(ones[:], 1.0)
            pool.memset(minus_half[:], -0.5).then_inc(ones_ready, 1)
            pool.dma_start(ident[:], identity).then_inc(small_landed, 16)
            pool.dma_start(lam_in[:], lambdas).then_inc(small_landed, 16)
            pool.dma_start(sub_gain_in[:], subln).then_inc(small_landed, 16)
            for g in range(4):
                pool.wait_ge(x_landed[g], 16)
                tiles = slice(4 * g, 4 * g + 4)
                pool.tensor_tensor(x0_sq[:, tiles, :], x[:, tiles, :], x[:, tiles, :], ALU.mult).then_inc(x0_squared, 1)
            for g in range(2):
                pool.wait_ge(x0_squared, 3 + g)
                a, b = (x0_sq[:, lo:lo + 4, :] for lo in (4 * g, 4 * g + 8))
                pool.tensor_tensor(a, a, b, ALU.add).then_inc(x0_summed, 1)
            pool.dma_start(wf[:], w_fnet.rearrange("g c e -> c g e")).then_inc(dft_landed, 16)
            pool.dma_start(ch_dft[:], channel_dft).then_inc(dft_landed, 16)
            pool.dma_start(pos_dft[:], position_dft).then_inc(dft_landed, 16)
            pool.wait_ge(ones_ready, 1)

            def token_inverse(n):
                pool.wait_ge(mean_ready, n + 1)
                pool.tensor_tensor(rstd_col[:], mean_sq[:], minus_half[:], ALU.pow).then_inc(inv_ready, 1)

            token_inverse(N_MIX0)
            token_inverse(N_FFN0)
            token_inverse(N_MIX1)
            with pool.Fori(0, C_HEADS) as h:
                pool.wait_ge(omean_ready, h + 1)
                pool.tensor_tensor(o_inv[:], o_mean[:], minus_half[:], ALU.pow).then_inc(oinv_ready, 1)
            token_inverse(N_FFN1)
            token_inverse(N_FINAL)
            pool.wait_ge(rstd_ready, N_FINAL + 1)
            pool.wait_ge(gx_hi, KT * 5)
            scale_rows(pool, *Y_LAST).then_inc(y_last_ready, 1)

        @block.scalar
        def _(act):
            def split_hi(n, o=0):
                u, part = n // 2, n % 2
                if n == 0:
                    act.wait_ge(first_half_landed, 16)
                elif part == 0 or n == 1:
                    act.wait_ge(raw_landed[u % RAW_SLOTS], 16 * (u // RAW_SLOTS + 1) + 16 // RAW_SLOTS * o)
                if n >= RING:
                    act.wait_ge(w_used, n - RING + 1 + 2 * o)
                act.activation(w_hi[:, n % RING, :], raw[:, u % RAW_SLOTS, part * HALF:(part + 1) * HALF],
                               ACT.Copy).then_inc(hi_ready, 1)

            def copy_cross(u, o):
                act.wait_ge(w_used, 2 * u + 2 + 2 * o)
                act.wait_ge(acc_free, u + o)
                act.activation(copied[:], acc_of(u)[:, SEQ:], ACT.Copy).then_inc(copy_ready, 1)

            def unit(u, o=0, before=(), first=(), second=(), copy=True, split=True):
                for step in before:
                    step()
                if split:
                    split_hi(2 * u + 4, o)
                for step in first:
                    step()
                if copy:
                    copy_cross(u, o)
                if split:
                    split_hi(2 * u + 5, o)
                for step in second:
                    step()

            def hi_gx(n, t):
                dst = y_out[:, t, :] if n == N_FINAL else gx[:, t, 0:SEQ]
                act.activation(dst, x[:, t, :], ACT.Copy, scale=gain[:, n, bass.ts(t, 1)]).then_inc(gx_hi, 1)

            def gx_part(n, f, of=0):
                t = f + of
                act.wait_ge(sum_steps, SUMS_BEFORE[n] + 1 + t)
                if n != N_FINAL:
                    hi_gx(n, t)
                act.activation(x_sq[:], x[:, t, :], ACT.Square).then_inc(xsq_done, 1)
                if n == N_FINAL:
                    hi_gx(n, t)

            def residual(n, u, f, o=0, of=0):
                def step():
                    act.wait_ge(acc_free, u + 1 + o)
                    gx_part(n, f, of)
                return step

            def exps(m, s, head, heads_before, os=0, oh=0):
                def step():
                    act.wait_ge(neg_ready, s + 1 + os)
                    act.wait_ge(attn_ready, QT * (heads_before + oh))
                    for t in range(QT):
                        act.activation(probs[:, m, t, :], logits[:, m, t, :], ACT.Exp,
                                       bias=neg_max[:, m, t:t + 1],
                                       accum_out=row_sum[:, m, t:t + 1]).then_inc(exp_done, 1)
                return step

            def copy_v(n, width, oh=0):
                def step():
                    act.wait_ge(vt_ready, n + 1 + oh)
                    act.wait_ge(o_ready, n + oh)
                    act.activation(v_tok[:, 0, :, 0:width], ps_v[:, :, 0:width], ACT.Copy).then_inc(v_copied, 1)
                return step

            def copy_attn(n, oh=0):
                def step():
                    act.wait_ge(pt_ready, n + 1 + oh)
                    act.wait_ge(o_ready, n + oh)
                    act.activation(attn_t[:, 0, :, :], ps_attn_t[:, :, ::-1], ACT.Copy).then_inc(pt_copied, 1)
                return step

            act.dma_start(tab[0:BUCKETS, :], table).then_inc(tab_landed, 16)
            act.dma_start(tab[BUCKETS:BUCKETS + 1, :], a_head_row).then_inc(tab_landed, 16)
            act.dma_start(one_hot, onehot).then_inc(tab_landed, 16)
            split_hi(0)
            act.wait_ge(gain_landed, 16)
            for f in range(KT):
                act.wait_ge(x_landed[f // 4], 16)
                hi_gx(N_MIX0, f)
                if f == 3:
                    split_hi(1)
                if f == 11:
                    act.wait_ge(line_ready, 1)
                    act.activation(line, ps_scores[0][0:HEADS, :, :].rearrange("h t k -> h (t k)"), ACT.Copy
                                   ).then_inc(line_copied, 1)
            split_hi(2)
            split_hi(3)
            split_hi(4)
            split_hi(5)
            copy_cross(0, 0)
            split_hi(6)
            split_hi(7)
            copy_cross(1, 0)

            def copy_maps():
                act.wait_ge(map_ready, 1)
                act.activation(ch_map[:, :, 0, :], ps_o[:].rearrange("p (g e) -> p g e", g=GROUPS), ACT.Copy)
                act.activation(ch_map[:, :, 1, :], ps_attn_t[:].rearrange("p t (g e) -> p (t g) e", e=P), ACT.Copy
                               ).then_inc(map_copied, 1)
                act.wait_ge(lam_sum_ready, 1)
                act.activation(lam_exp[:], ps_v[:, 0, 0:2], ACT.Exp).then_inc(lam_exp_ready, 1)

            def hi_att0(h, oh):
                def step():
                    act.wait_ge(o_ready, h + 1 + oh)
                    act.activation(mid[:, h + oh, 0:SEQ], ps_o[:, 0:SEQ], ACT.Copy).then_inc(mid_hi, 1)
                return step

            def copy_mixed(g):
                def step():
                    act.wait_ge(mix1_ready, g + 1)
                    act.wait_ge(mix2_ready, g)
                    act.activation(mixed[:], ps_scores[1][:], ACT.Copy).then_inc(mix_copied, 1)
                return step

            def hi_mix(g):
                def step():
                    act.wait_ge(mix2_ready, g + 1)
                    act.activation(mid[:, A_HEADS + g, 0:SEQ], ps_aux[:, 0:SEQ], ACT.Copy).then_inc(mid_hi, 1)
                return step

            def head0(h, oh=0):
                u, o = 2 + 3 * h, 3 * oh
                if h == 0:
                    unit(u)
                    unit(u + 1, first=[exps(0, 0, 0, 0)], second=[copy_maps])
                    unit(u + 2, second=[copy_v(0, P), copy_attn(0)])
                    return
                unit(u, o, first=[exps(0, h, h, h, oh, oh)], second=[hi_att0(0, 0)] if h == 1 else [])
                unit(u + 1, o, second=[copy_v(h, P, oh), copy_attn(h, oh)])
                if h < A_HEADS - 1:
                    unit(u + 2, o, second=[hi_att0(h, oh)])
                else:
                    unit(u + 2, o, first=[copy_mixed(0)], second=[hi_att0(h, oh), hi_mix(0)])

            head0(0)
            head0(1)
            with act.Fori(0, 2) as i:
                for h in range(2, 6):
                    head0(h, 4 * i)
            for h in range(10, A_HEADS):
                head0(h)
            for g in (1, 2):
                unit(U_OUT0 - 3 + g, first=[copy_mixed(g)], second=[hi_mix(g)])

            def out_projection(u0, n, before=(), first=(), second=()):
                for step in before:
                    step()
                split_hi(2 * u0 + 4)
                for step in first:
                    step()
                split_hi(2 * u0 + 5)
                for step in second:
                    step()
                split_hi(2 * u0 + 6)
                residual(n, u0, 0)()
                split_hi(2 * u0 + 7)
                residual(n, u0 + 1, 1)()
                for f in (2, 3):
                    unit(u0 + f, copy=False, second=[residual(n, u0 + f, f)])
                with act.Fori(1, 4) as i:
                    for s in range(4):
                        unit(u0 + s, 4 * i, copy=False, second=[residual(n, u0 + s, s, 4 * i, 4 * i)])

            out_projection(U_OUT0, N_FFN0, first=[copy_mixed(3)], second=[hi_mix(3)])
            load_bias(act, bias_second, A_HEADS, 0, C_HEADS)

            def hidden(u, f, k, o=0, of=0, ok=0, chunk=0):
                def hi_hidden():
                    act.wait_ge(squared, k + 1 + ok)
                    act.activation(mid[:, f + of, 0:SEQ], square[:], ACT.Copy).then_inc(mid_hi, 1)
                unit(u, o, second=[hi_hidden])

            def output(u, f, k, o=0, of=0, ok=0, chunk=0):
                unit(u, o, copy=False)

            def last_output(n):
                def run(u, f, k, o=0, of=0, ok=0, chunk=0):
                    unit(u, o, copy=False, second=[residual(n, u, f, o, of)], split=u + 2 < UNITS)
                return run

            feed_forward(act, 0, U_FF0, hidden, output, last_output(N_MIX1))

            unit(U_QKV1)
            unit(U_QKV1 + 1)

            def squares(h, oh=0):
                def step():
                    act.wait_ge(o_ready, A_HEADS + h + 1 + oh)
                    act.wait_ge(osq_done, QT * (h + oh))
                    for t in range(QT):
                        act.activation(o_sq[:, t, :], ps_o[:, t * SEQ:(t + 1) * SEQ], ACT.Square,
                                       accum_out=o_sum[:, t:t + 1]).then_inc(osq_done, 1)
                return step

            def hi_att1(h, oh=0):
                def step():
                    act.wait_ge(ot_ready, h + 1 + oh)
                    for j in range(2):
                        act.activation(mid[:, 2 * h + j + 2 * oh, 0:SEQ], ps_aux[:, j * SEQ:(j + 1) * SEQ], ACT.Copy,
                                       scale=sub_gain[:, j:j + 1]).then_inc(mid_hi, 1)
                return step

            def head1(h, oh=0):
                u, o, g = U_QKV1 + 2 + 6 * h, 6 * oh, A_HEADS + h
                unit(u, o, first=[exps(0, A_HEADS + 2 * h, h, g, 2 * oh, oh)])
                unit(u + 1, o)
                unit(u + 2, o, first=[exps(1, A_HEADS + 2 * h + 1, h, g, 2 * oh, oh)])
                unit(u + 3, o, second=[copy_attn(g, oh)])
                if h < C_HEADS - 1:
                    unit(u + 4, o, first=[copy_v(g, 2 * P, oh)])
                    unit(u + 5, o, before=[squares(h, oh)], second=[hi_att1(h, oh)])

            head1(0)
            with act.Fori(0, 3) as i:
                for h in (1, 2):
                    head1(h, 2 * i)
            head1(7)
            out_projection(U_OUT1, N_FFN1, before=[copy_v(HEADS - 1, 2 * P)], first=[squares(C_HEADS - 1)],
                           second=[hi_att1(C_HEADS - 1)])
            feed_forward(act, 1, U_FF1, hidden, output, last_output(N_FINAL))

        @block.vector
        def _(dve):
            def split_lo(n, o=0):
                u, part = n // 2, n % 2
                dve.wait_ge(hi_ready, n + 1 + 2 * o)
                dve.tensor_tensor(w_lo[:, n % RING, :], raw[:, u % RAW_SLOTS, part * HALF:(part + 1) * HALF],
                                  w_hi[:, n % RING, :].bitcast(F32), ALU.subtract).then_inc(lo_ready, 1)

            def sum_product(u, c, o=0, oc=0):
                dve.wait_ge(copy_ready, c + 1 + oc)
                dve.tensor_tensor(summed[:], acc_of(u)[:, 0:SEQ], copied[:], ALU.add).then_inc(acc_free, 1)
                dve.wait_ge(acc_free, u + 1 + o)

            def projected(u, c, dst, scale=1.0, o=0, oc=0):
                def step():
                    p = c if u < U_OUT0 else c - FF_CHUNKS * KT
                    dve.wait_ge(proj_ready, p + oc)
                    sum_product(u, c, o, oc)
                    dve.scalar_tensor_tensor(dst, summed[:], scale, rstd[:], ALU.mult, ALU.mult
                                             ).then_inc(proj_ready, 1)
                return step

            def projected_split(u, c, dst, n, scale=1.0, o=0, oc=0, on=0):
                full = projected(u, c, proj_full[:], scale, o, oc)

                def step():
                    if n:
                        dve.wait_ge(qk_ready, n + on)
                    full()
                    p = c if u < U_OUT0 else c - FF_CHUNKS * KT
                    dve.wait_ge(proj_ready, p + 1 + oc)
                    dve.tensor_copy(dst[:, 0, :], proj_full[:]).then_inc(qk_hi, 1)
                    dve.wait_ge(qk_hi, n + 1 + on)
                    dve.tensor_tensor(dst[:, 1, :], proj_full[:], dst[:, 0, :].bitcast(F32), ALU.subtract
                                      ).then_inc(qk_ready, 1)
                return step

            def lo_v(n, width, oh=0):
                def step():
                    dve.wait_ge(v_copied, n + 1 + oh)
                    dve.tensor_tensor(v_tok[:, 1, :, 0:width], ps_v[:, :, 0:width],
                                      v_tok[:, 0, :, 0:width].bitcast(F32), ALU.subtract).then_inc(v_split, 1)
                return step

            def lo_attn(n, oh=0):
                def step():
                    dve.wait_ge(pt_copied, n + 1 + oh)
                    dve.tensor_tensor(attn_t[:, 1, :, :], ps_attn_t[:, :, ::-1], attn_t[:, 0, :, :].bitcast(F32),
                                      ALU.subtract).then_inc(pt_split, 1)
                return step

            def add_to_residual(u, f, r, o=0, of=0, r_o=0, late=0):
                def step():
                    t = f + of
                    dve.wait_ge(w_used, 2 * u + 2 + late + 2 * o)
                    dve.tensor_tensor(x[:, t, :], x[:, t, :], acc_of(u)[:, 0:SEQ], ALU.add).then_inc(acc_half, 1)
                    dve.wait_ge(acc_half, r + 1 + r_o)
                    dve.tensor_tensor(x[:, t, :], x[:, t, :], acc_of(u)[:, SEQ:], ALU.add).then_inc(acc_free, 1)
                return step

            def lo_gx(n, t):
                dve.wait_ge(gx_hi, KT * n + t + 1)
                dve.scalar_tensor_tensor(gx[:, t, SEQ:], x[:, t, :], gain[:, n, bass.ts(t, 1)],
                                         gx[:, t, 0:SEQ].bitcast(F32), ALU.mult, ALU.subtract).then_inc(gx_ready, 1)

            def gx_rest(n, f, of=0):
                def step():
                    t = f + of
                    if n != N_FINAL:
                        lo_gx(n, t)
                    dve.wait_ge(xsq_done, SQUARES_BEFORE[n] + t + 1)
                    dve.wait_ge(sum_steps, SUMS_BEFORE[n] + 1 + t)
                    dve.tensor_tensor(sum_sq[:], sum_sq[:], x_sq[:], ALU.add).then_inc(sum_steps, 1)
                return step

            def clear_sum(m=None):
                if m is not None:
                    dve.wait_ge(mid_ready, m)
                dve.memset(sum_sq[:], 0.0).then_inc(sum_steps, 1)

            def unit(u, evac, o=0, before=(), first=(), then=(), second=(), split=True):
                for step in before:
                    step()
                if split:
                    split_lo(2 * u + 4, o)
                for step in first:
                    step()
                evac()
                for step in then:
                    step()
                if split:
                    split_lo(2 * u + 5, o)
                for step in second:
                    step()

            def token_stats(n):
                dve.wait_ge(stat_ready, n + 1)
                dve.tensor_scalar(mean_sq[:], ps_aux[:, 0:QT], 1.0 / D, EPS, ALU.mult, ALU.add
                                  ).then_inc(mean_ready, 1)
                dve.wait_ge(inv_ready, n + 1)
                for t in range(QT):
                    dve.tensor_scalar(diag[:, t, :], ident[:], rstd_col[:, t:t + 1], None, ALU.mult
                                      ).then_inc(diag_ready, 1)

            def token_rstd(n):
                dve.wait_ge(bcast_ready, n + 1)
                dve.tensor_copy(rstd[:], ps_aux[:, 0:SEQ]).then_inc(rstd_ready, 1)
                dve.wait_ge(rstd_ready, n + 1)

            def first_unit(u, n, evac, second=()):
                split_lo(2 * u + 4)
                token_stats(n)
                split_lo(2 * u + 5)
                token_rstd(n)
                evac()
                for step in second:
                    step()

            def score_rows(m, s, before, head, os=0, ob=0, oh=0):
                def step():
                    dve.wait_ge(scores_ready, s + 1 + os)
                    dve.wait_ge(exp_done, before + ob)
                    dve.tensor_tensor(logits[:, m, :, :], ps_scores[m][:], bias[:, head + oh, :, :], ALU.add
                                      ).then_inc(scores_read, 1)
                    dve.wait_ge(scores_read, s + 1 + os)
                    dve.tensor_reduce(row_max[:, m, :], logits[:, m, :, :], AX_X, ALU.max).then_inc(max_done, 1)
                    dve.wait_ge(max_done, s + 1 + os)
                    dve.tensor_scalar(neg_max[:, m, :], row_max[:, m, :], -1.0, None, ALU.mult
                                      ).then_inc(neg_ready, 1)
                return step

            split_lo(0)
            dve.wait_ge(gain_landed, 16)
            for f in range(KT):
                dve.wait_ge(x_landed[f // 4], 16)
                lo_gx(N_MIX0, f)
                if f == 3:
                    split_lo(1)
            split_lo(2)
            split_lo(3)
            dve.wait_ge(small_landed, 16 * 3)
            dve.tensor_tensor(lam_prod[:], lam_in[:, 0:4:2], lam_in[:, 1:4:2], ALU.mult).then_inc(lam_steps, 1)
            dve.tensor_scalar(sub_gain[:], sub_gain_in[:], 1.0 - LAMBDA_INIT, None, ALU.mult).then_inc(lam_steps, 1)
            split_lo(4)
            split_lo(5)
            n, steps = KT // 2, 2
            while n > 1:
                n //= 2
                dst = x0_sq[:, 0:n, :] if n > 1 else sum_sq[:]
                a, b = (x0_sq[:, k * n:(k + 1) * n, :] for k in range(2))
                if n == 1:
                    a, b = x0_sq[:, 0, :], x0_sq[:, 1, :]
                dve.wait_ge(x0_summed, steps)
                dve.tensor_tensor(dst, a, b, ALU.add).then_inc(x0_summed, 1)
                steps += 1

            def negative_lambda():
                dve.wait_ge(lam_exp_ready, 1)
                dve.tensor_tensor(lam_diff[:], lam_exp[:, 1:2], lam_exp[:, 0:1], ALU.subtract).then_inc(lam_steps, 1)
                dve.wait_ge(lam_steps, 3)
                dve.tensor_scalar(neg_lam[:], lam_diff[:], -LAMBDA_INIT, None, ALU.add).then_inc(lam_steps, 1)

            q, k, v0 = q_t[:, :, ::-1], k_t[:], v_t[:, 0, :]
            token_stats(N_MIX0)
            split_lo(6)
            token_rstd(N_MIX0)
            projected_split(0, 0, q, 0, SCALE)()
            projected_split(1, 1, k, 1)()
            split_lo(7)

            def normalise(h, oh=0):
                def step():
                    dve.wait_ge(exp_done, QT * (h + 1) + QT * oh)
                    dve.wait_ge(attn_ready, QT * (h + oh))
                    dve.reciprocal(row_inv[:, 0, :], row_sum[:, 0, :]).then_inc(soft_steps, 1)
                    dve.wait_ge(soft_steps, h + 1 + oh)
                    dve.wait_ge(pt_ready, h + oh)
                    for t in range(QT):
                        dve.tensor_scalar(attn[:, t, :], probs[:, 0, t, :], row_inv[:, 0, t:t + 1], None, ALU.mult
                                          ).then_inc(attn_ready, 1)
                return step

            def lo_part(tile, src, ot=0):
                def step():
                    dve.wait_ge(mid_hi, tile + 1 + ot)
                    dve.tensor_tensor(mid[:, tile + ot, SEQ:], src, mid[:, tile + ot, 0:SEQ].bitcast(F32),
                                      ALU.subtract).then_inc(mid_ready, 1)
                return step

            def head0(h, oh=0):
                u, o = 2 + 3 * h, 3 * oh
                last = h == A_HEADS - 1
                if h == 0:
                    unit(u, projected(u, u, v0))
                    unit(u + 1, projected_split(u + 1, u + 1, q, 2, SCALE),
                         first=[lambda: dve.wait_ge(bias_first, 16 * QT), score_rows(0, 0, 0, 0)],
                         then=[normalise(0)])
                    unit(u + 2, projected_split(u + 2, u + 2, k, 3),
                         then=[lo_v(0, P), lo_attn(0)])
                    return
                unit(u, projected(u, u, v0, 1.0, o, o), o,
                     first=[score_rows(0, h, QT * h, h, oh, QT * oh, oh), normalise(h, oh)],
                     second=[lo_part(0, ps_o[:, 0:SEQ])] if h == 1 else [])
                attention_lo = [lo_v(h, P, oh), lo_attn(h, oh)]
                attended_lo = lo_part(h, ps_o[:, 0:SEQ], oh)
                if last:
                    unit(u + 1, projected(u + 1, u + 1, u_t), then=attention_lo)
                    unit(u + 2, projected(u + 2, u + 2, u_t),
                         second=[attended_lo, lo_part(A_HEADS, ps_aux[:, 0:SEQ])])
                else:
                    unit(u + 1, projected_split(u + 1, u + 1, q, 2 * h + 2, SCALE, o, o, 2 * oh), o,
                         then=attention_lo)
                    unit(u + 2, projected_split(u + 2, u + 2, k, 2 * h + 3, 1.0, o, o, 2 * oh), o,
                         second=[attended_lo])

            head0(0)
            negative_lambda()
            head0(1)
            dve.wait_ge(bias_rest, 16 * QT)
            with dve.Fori(0, 2) as i:
                for h in range(2, 6):
                    head0(h, 4 * i)
            for h in range(10, A_HEADS):
                head0(h)
            for g in (1, 2):
                u = U_OUT0 - 3 + g
                unit(u, projected(u, u, u_t), second=[lo_part(A_HEADS + g, ps_aux[:, 0:SEQ])])

            def out_projection(u0, n, r, before=(), first=(), second=()):
                clear_sum()
                for step in before:
                    step()
                split_lo(2 * u0 + 4)
                for step in first:
                    step()
                split_lo(2 * u0 + 5)
                for step in second:
                    step()
                add_to_residual(u0, 0, r, late=1)()
                split_lo(2 * u0 + 6)
                gx_rest(n, 0)()
                add_to_residual(u0 + 1, 1, r + 1)()
                split_lo(2 * u0 + 7)
                gx_rest(n, 1)()
                for f in (2, 3):
                    unit(u0 + f, add_to_residual(u0 + f, f, r + f), second=[gx_rest(n, f)])
                with dve.Fori(1, 4) as i:
                    for s in range(4):
                        unit(u0 + s, add_to_residual(u0 + s, s, r + s, 4 * i, 4 * i, 4 * i), 4 * i,
                             second=[gx_rest(n, s, 4 * i)])

            out_projection(U_OUT0, N_FFN0, 0, second=[lo_part(KT - 1, ps_aux[:, 0:SEQ])])

            def hidden_in(layer):
                c0 = (COPIES_FF0, COPIES_FF1)[layer]
                m0 = (MID_FF0, MID_FF1)[layer]
                k0 = layer * FF_CHUNKS * KT

                def run(u, f, k, o=0, of=0, ok=0, chunk=0):
                    c, k_in = c0 + k - k0, k

                    def evac():
                        sum_product(u, c, o, ok)
                        dve.scalar_tensor_tensor(relu[:], summed[:], 0.0, rstd[:], ALU.max, ALU.mult
                                                 ).then_inc(relu_done, 1)
                        dve.wait_ge(relu_done, k_in + 1 + ok)
                        dve.wait_ge(mid_ready, m0 + k - k0 + ok)
                        dve.tensor_tensor(square[:], relu[:], relu[:], ALU.mult).then_inc(squared, 1)

                    def lo_hidden():
                        dve.wait_ge(mid_hi, m0 + k - k0 + 1 + ok)
                        dve.tensor_tensor(mid[:, f + of, SEQ:], square[:], mid[:, f + of, 0:SEQ].bitcast(F32),
                                          ALU.subtract).then_inc(mid_ready, 1)

                    if f == 0 and isinstance(o, int) and u in (U_FF0, U_FF1):
                        first_unit(u, (N_FFN0, N_FFN1)[layer], evac, second=[lo_hidden])
                    else:
                        unit(u, evac, o, second=[lo_hidden])
                return run

            def output_in(r0, layer):
                def run(u, f, k, o=0, of=0, ok=0, chunk=0):
                    r = r0 + k - layer * FF_CHUNKS * KT
                    unit(u, add_to_residual(u, f, r, o, of, ok), o)
                return run

            def last_output_in(r0, layer, n):
                def run(u, f, k, o=0, of=0, ok=0, chunk=0):
                    r = r0 + k - layer * FF_CHUNKS * KT
                    unit(u, add_to_residual(u, f, r, o, of, ok), o, second=[gx_rest(n, f, of)],
                         split=u + 2 < UNITS)
                return run

            dve.wait_ge(proj_ready, U_OUT0)
            feed_forward(dve, 0, U_FF0, hidden_in(0), output_in(KT, 0), last_output_in(KT, 0, N_MIX1),
                         lambda: clear_sum(MID_ATT1))

            first_unit(U_QKV1, N_MIX1, projected_split(U_QKV1, COPIES_QKV1, q, 2 * A_HEADS, SCALE))
            unit(U_QKV1 + 1, projected_split(U_QKV1 + 1, COPIES_QKV1 + 1, k, 2 * A_HEADS + 1))
            dve.wait_ge(bias_second, 16 * QT)
            dve.wait_ge(lam_steps, 4)

            def combine(h, oh=0):
                def step():
                    n = A_HEADS + 4 * h
                    dve.wait_ge(exp_done, QT * A_HEADS + 4 * (h + 1) + 4 * oh)
                    dve.wait_ge(attn_ready, QT * (A_HEADS + h + oh))
                    dve.reciprocal(row_inv[:], row_sum[:]).then_inc(soft_steps, 1)
                    dve.wait_ge(soft_steps, n + 1 + 4 * oh)
                    dve.tensor_scalar(lam_inv[:], row_inv[:, 1, :], neg_lam[:], None, ALU.mult
                                      ).then_inc(soft_steps, 1)
                    for t in range(QT):
                        dve.tensor_scalar(part0[:, t, :], probs[:, 0, t, :], row_inv[:, 0, t:t + 1], None, ALU.mult
                                          ).then_inc(soft_steps, 1)
                    dve.wait_ge(soft_steps, n + 4 + 4 * oh)
                    dve.wait_ge(pt_ready, A_HEADS + h + oh)
                    for t in range(QT):
                        dve.scalar_tensor_tensor(attn[:, t, :], probs[:, 1, t, :], lam_inv[:, t:t + 1],
                                                 part0[:, t, :], ALU.mult, ALU.add).then_inc(attn_ready, 1)
                return step

            def head_norm(h, oh=0):
                def step():
                    dve.wait_ge(osq_done, QT * (h + 1 + oh))
                    dve.tensor_scalar(o_mean[:], o_sum[:], 1.0 / (2 * P), EPS, ALU.mult, ALU.add
                                      ).then_inc(omean_ready, 1)
                    dve.wait_ge(oinv_ready, h + 1 + oh)
                    dve.wait_ge(ot_ready, h + oh)
                    for t in range(QT):
                        dve.tensor_scalar(o_norm[:, t, :], ps_o[:, t * SEQ:(t + 1) * SEQ], o_inv[:, t:t + 1], None,
                                          ALU.mult).then_inc(onorm_ready, 1)
                return step

            def lo_att1(h, oh=0):
                def step():
                    dve.wait_ge(mid_hi, MID_ATT1 + 2 * (h + 1) + 2 * oh)
                    for j in range(2):
                        t = 2 * h + j + 2 * oh
                        dve.scalar_tensor_tensor(mid[:, t, SEQ:], ps_aux[:, j * SEQ:(j + 1) * SEQ],
                                                 sub_gain[:, j:j + 1], mid[:, t, 0:SEQ].bitcast(F32),
                                                 ALU.mult, ALU.subtract).then_inc(mid_ready, 1)
                return step

            def head1(h, oh=0):
                u, c = U_QKV1 + 2 + 6 * h, COPIES_QKV1 + 2 + 6 * h
                o, s, e = 6 * oh, A_HEADS + 2 * h, QT * A_HEADS + 4 * h

                n = 2 * A_HEADS + 4 * h + 2

                def proj(j, dst):
                    return projected(u + j, c + j, dst, 1.0, o, o)

                def proj_split(j, dst, m, scale=1.0):
                    return projected_split(u + j, c + j, dst, m, scale, o, o, 4 * oh)

                unit(u, proj_split(0, q, n, SCALE), o, first=[score_rows(0, s, e, h, 2 * oh, 4 * oh, oh)])
                unit(u + 1, proj_split(1, k, n + 1), o)
                unit(u + 2, proj(2, v_t[:, 0, :]), o,
                     first=[score_rows(1, s + 1, e, h, 2 * oh, 4 * oh, oh), combine(h, oh)])
                unit(u + 3, proj(3, v_t[:, 1, :]), o, then=[lo_attn(A_HEADS + h, oh)])
                if h < C_HEADS - 1:
                    unit(u + 4, proj_split(4, q, n + 2, SCALE), o, first=[lo_v(A_HEADS + h, 2 * P, oh)])
                    unit(u + 5, proj_split(5, k, n + 3), o, before=[head_norm(h, oh)], second=[lo_att1(h, oh)])

            head1(0)
            with dve.Fori(0, 3) as i:
                for h in (1, 2):
                    head1(h, 2 * i)
            head1(7)
            out_projection(U_OUT1, N_FFN1, KT * (1 + FF_CHUNKS), before=[lo_v(HEADS - 1, 2 * P)], first=[head_norm(C_HEADS - 1)],
                           second=[lo_att1(C_HEADS - 1)])
            dve.wait_ge(proj_ready, U_OUT0 + 6 * C_HEADS)
            feed_forward(dve, 1, U_FF1, hidden_in(1), output_in(KT * (2 + FF_CHUNKS), 1),
                         last_output_in(KT * (2 + FF_CHUNKS), 1, N_FINAL),
                         lambda: clear_sum(MID_FF1 + KT * FF_CHUNKS))

            token_stats(N_FINAL)
            token_rstd(N_FINAL)
            dve.wait_ge(gx_hi, KT * 5)
            for lo, hi in Y_GROUPS:
                scale_rows(dve, lo, hi).then_inc(y_ready, 1)

        @block.tensor
        def _(pe):
            def half(n, u, kts, operand, o=0, hooks=None, whole=None, tile_wait=None):
                hooks = hooks or {}
                pe.wait_ge(lo_ready, n + 1 + 2 * o)
                for j, kt in enumerate(kts):
                    for step in hooks.get(j, ()):
                        step()
                    if tile_wait is not None:
                        ready, base, first = tile_wait
                        if kt == 0 or kt >= first:
                            pe.wait_ge(ready, base + (kt + 1 if kt else first))
                    cols = slice(j * P, (j + 1) * P)

                    def hi():
                        return pe.matmul(acc_of(u)[:], w_hi[:, n % RING, cols], operand[:, kt, :], start=kt == 0,
                                         stop=kt == KT - 1)

                    def lo():
                        return pe.matmul(acc_of(u)[:, SEQ:], w_lo[:, n % RING, cols], operand[:, kt, 0:SEQ],
                                         start=False, stop=False)

                    if kt == KT - 1:
                        lo()
                        ins = hi()
                    else:
                        hi()
                        ins = lo()
                ins.then_inc(w_used, 1)
                for step in hooks.get(KT // 2, ()):
                    step()

            FIRST, SECOND = range(0, KT // 2), range(KT // 2, KT)

            def unit(u, operand, o=0, hooks=({}, {}), tile_wait=None):
                if u >= 3:
                    pe.wait_ge(acc_free, u - 1 + o)
                half(2 * u, u, FIRST, operand, o, hooks[0], tile_wait=tile_wait)
                half(2 * u + 1, u, SECOND, operand, o, hooks[1], tile_wait=tile_wait)

            def stat_sum(n):
                def step():
                    if n == N_MIX0:
                        pe.wait_ge(x0_summed, 2 + int(math.log2(KT // 2)))
                    else:
                        pe.wait_ge(sum_steps, SUMS_BEFORE[n + 1])
                    for t in range(QT):
                        ins = pe.matmul(ps_aux[:, t:t + 1], sum_sq[:, t * P:(t + 1) * P], ones[:, 0:1],
                                        start=True, stop=True)
                    ins.then_inc(stat_ready, 1)
                return step

            def stat_spread(n):
                def step():
                    pe.wait_ge(diag_ready, QT * (n + 1))
                    for t in range(QT):
                        ins = pe.matmul(ps_aux[:, t * P:(t + 1) * P], ones[:], diag[:, t, :], start=True, stop=True)
                    ins.then_inc(bcast_ready, 1)
                return step

            def split_matmul(out, lhsT, rhs, start, stop):
                for i, (a, b) in enumerate(((0, 1), (1, 0), (0, 0))):
                    ins = pe.matmul(out, lhsT(a), rhs(b), start=start and i == 0, stop=stop and i == 2)
                return ins

            def scores(m, n, read, on=0, orr=0):
                def step():
                    pe.wait_ge(qk_ready, n + on)
                    pe.wait_ge(scores_read, read + orr)
                    for t in range(QT):
                        ins = split_matmul(ps_scores[m][:, t, :], lambda a: q_t[:, a, t * P:(t + 1) * P],
                                           lambda b: k_t[:, b, :], True, True)
                    ins.then_inc(scores_ready, 1)
                return step

            def turn_v(n, proj, tiles, oh=0, op=0):
                def step():
                    pe.wait_ge(proj_ready, proj + op)
                    pe.wait_ge(v_split, n + oh)
                    for kt in range(QT):
                        for j in range(tiles):
                            ins = pe.transpose(ps_v[:, kt, j * P:(j + 1) * P], v_t[:, j, kt * P:(kt + 1) * P], ident[:])
                    ins.then_inc(vt_ready, 1)
                return step

            def turn_attn(n, oh=0):
                def step():
                    pe.wait_ge(attn_ready, QT * (n + 1) + QT * oh)
                    pe.wait_ge(pt_split, n + oh)
                    for kt in range(QT):
                        for t in range(QT):
                            ins = pe.transpose(ps_attn_t[:, kt, t * P:(t + 1) * P], attn[:, t, kt * P:(kt + 1) * P],
                                               ident[:])
                    ins.then_inc(pt_ready, 1)
                return step

            def attend0(h, oh=0):
                def step():
                    pe.wait_ge(v_split, h + 1 + oh)
                    pe.wait_ge(pt_split, h + 1 + oh)
                    pe.wait_ge(mid_ready, h + oh)
                    for kt in range(QT):
                        ins = split_matmul(ps_o[:, 0:SEQ], lambda a: v_tok[:, a, kt, 0:P],
                                           lambda b: attn_t[:, b, kt, :], kt == 0, kt == QT - 1)
                    ins.then_inc(o_ready, 1)
                return step

            def mix_channels(g):
                def step():
                    pe.wait_ge(proj_ready, 3 * A_HEADS + g + 1)
                    pe.wait_ge(mix_copied, g)
                    for t in range(QT):
                        ins = pe.matmul(ps_scores[1][:, t, :], u_t[:, t * P:(t + 1) * P],
                                        ch_map[:, g, :, :].rearrange("p r e -> p (r e)"), start=True, stop=True)
                    ins.then_inc(mix1_ready, 1)
                return step

            def mix_positions(g):
                def step():
                    pe.wait_ge(mix_copied, g + 1)
                    if g:
                        pe.wait_ge(mid_ready, A_HEADS + g)
                    for t in range(QT):
                        for r in range(2):
                            ins = pe.matmul(ps_aux[:, 0:SEQ], mixed[:, t, r * P:(r + 1) * P], pos_dft[:, t, r, :],
                                            start=t == r == 0, stop=t == r == 1)
                    ins.then_inc(mix2_ready, 1)
                return step

            pe.wait_ge(ones_ready, 1)
            pe.wait_ge(tab_landed, 16 * 3)
            pe.matmul(ps_scores[0][0:HEADS, :, :].rearrange("p t k -> p (t k)"), tab[:], one_hot, start=True,
                      stop=True).then_inc(line_ready, 1)

            def group_maps():
                pe.wait_ge(dft_landed, 16 * 3)
                for r, bank in enumerate((ps_o[:], ps_attn_t[:].rearrange("p t k -> p (t k)"))):
                    for g in range(GROUPS):
                        ins = pe.matmul(bank[:, g * P:(g + 1) * P], ch_dft[:, r, :], wf[:, g, :], start=True, stop=True)
                ins.then_inc(map_ready, 1)
                pe.wait_ge(lam_steps, 1)
                pe.matmul(ps_v[:, 0, 0:2], ones[:], lam_prod[:], start=True, stop=True).then_inc(lam_sum_ready, 1)
                pe.wait_ge(small_landed, 16 * 3)

            unit(0, gx, tile_wait=(gx_ready, 0, 1))
            unit(1, gx)

            def first_scores():
                pe.wait_ge(line_copied, 1)
                scores(0, 2, 0)()

            def first_turn():
                pe.wait_ge(map_copied, 1)
                pe.wait_ge(lam_exp_ready, 1)
                turn_v(0, 3, 1)()
                turn_attn(0)()

            def head0(h, oh=0):
                u, o = 2 + 3 * h, 3 * oh
                if h == 0:
                    unit(u, gx, hooks=({4: [stat_sum(N_MIX0)]}, {2: [stat_spread(N_MIX0)]}))
                    unit(u + 1, gx, hooks=({8: [first_scores]}, {4: [group_maps]}))
                    unit(u + 2, gx, hooks=({}, {4: [first_turn]}))
                    return
                unit(u, gx, o, hooks=({8: [scores(0, 2 * h + 2, h, 2 * oh, oh)]}, {4: [attend0(0)]} if h == 1 else {}))
                unit(u + 1, gx, o, hooks=({}, {4: [turn_v(h, u + 1, 1, oh, o), turn_attn(h, oh)]}))
                if h < A_HEADS - 1:
                    unit(u + 2, gx, o, hooks=({}, {4: [attend0(h, oh)]}))
                else:
                    unit(u + 2, gx, o, hooks=({8: [mix_channels(0)]}, {4: [attend0(h, oh)], 8: [mix_positions(0)]}))

            head0(0)
            head0(1)
            with pe.Fori(0, 2) as i:
                for h in range(2, 6):
                    head0(h, 4 * i)
            for h in range(10, A_HEADS):
                head0(h)
            for g in (1, 2):
                unit(U_OUT0 - 3 + g, gx, hooks=({8: [mix_channels(g)]}, {8: [mix_positions(g)]}))

            def out_projection(u0, mid0, hooks):
                pe.wait_ge(acc_free, u0 - 1)
                half(2 * u0, u0, FIRST, mid, hooks=hooks[0], tile_wait=(mid_ready, mid0, KT // 2))
                pe.wait_ge(acc_free, u0)
                half(2 * u0 + 1, u0 + 1, FIRST, mid, hooks=hooks[1])
                half(2 * u0 + 2, u0, SECOND, mid, hooks=hooks[2], tile_wait=(mid_ready, mid0, KT // 2))
                half(2 * u0 + 3, u0 + 1, SECOND, mid)
                for f in (2, 3):
                    unit_in_pairs(u0 + f)
                with pe.Fori(1, 4) as i:
                    for s in range(4):
                        unit(u0 + s, mid, 4 * i)

            def unit_in_pairs(u):
                unit(u, mid)

            out_projection(U_OUT0, MID_ATT0, ({8: [mix_channels(3)]}, {8: [mix_positions(3)]}, {}))

            def hidden(u, f, k, o=0, of=0, ok=0, chunk=0):
                if u in (U_FF0, U_FF1) and isinstance(o, int):
                    n = N_FFN0 if u == U_FF0 else N_FFN1
                    unit(u, gx, tile_wait=(gx_ready, GX_BEFORE[n], KT // 2), hooks=({}, {4: [stat_sum(n)]}))
                elif u in (U_FF0 + 1, U_FF1 + 1) and isinstance(o, int):
                    n = N_FFN0 if u == U_FF0 + 1 else N_FFN1
                    unit(u, gx, hooks=({4: [stat_spread(n)]}, {}))
                else:
                    unit(u, gx, o)

            def output(u, f, k, o=0, of=0, ok=0, chunk=0):
                layer = k // (FF_CHUNKS * KT)
                base = (MID_FF0, MID_FF1)[layer] + (k - f) - layer * FF_CHUNKS * KT
                unit(u, mid, o, tile_wait=(mid_ready, base + chunk, KT // 2) if f == 0 else None)

            feed_forward(pe, 0, U_FF0, hidden, output, output)

            unit(U_QKV1, gx, tile_wait=(gx_ready, GX_BEFORE[N_MIX1], KT // 2), hooks=({}, {4: [stat_sum(N_MIX1)]}))
            unit(U_QKV1 + 1, gx, hooks=({4: [stat_spread(N_MIX1)]}, {}))

            def attend1(h, oh=0):
                def step():
                    n = A_HEADS + h
                    pe.wait_ge(v_split, n + 1 + oh)
                    pe.wait_ge(pt_split, n + 1 + oh)
                    for t in range(QT):
                        for kt in range(QT):
                            ins = split_matmul(ps_o[:, t * SEQ:(t + 1) * SEQ],
                                               lambda a: attn_t[:, a, kt, t * P:(t + 1) * P],
                                               lambda b: v_tok[:, b, kt, :], kt == 0, kt == QT - 1)
                    ins.then_inc(o_ready, 1)
                return step

            def turn_output(h, oh=0):
                def step():
                    pe.wait_ge(onorm_ready, QT * (h + 1) + QT * oh)
                    pe.wait_ge(mid_ready, MID_ATT1 + 2 * h + 2 * oh)
                    for j in range(2):
                        for t in range(QT):
                            ins = pe.transpose(ps_aux[:, j * SEQ + t * P:j * SEQ + (t + 1) * P],
                                               o_norm[:, t, j * P:(j + 1) * P], ident[:])
                    ins.then_inc(ot_ready, 1)
                return step

            def head1(h, oh=0):
                u, o, n = U_QKV1 + 2 + 6 * h, 6 * oh, A_HEADS + h
                p, read, qk = U_OUT0 + 2 + 6 * h, A_HEADS + 2 * h, 2 * A_HEADS + 4 * h
                unit(u, gx, o, hooks=({8: [scores(0, qk + 2, read, 4 * oh, 2 * oh)]}, {}))
                unit(u + 1, gx, o)
                unit(u + 2, gx, o, hooks=({8: [scores(1, qk + 4, read, 4 * oh, 2 * oh)]}, {}))
                unit(u + 3, gx, o, hooks=({}, {4: [turn_attn(n, oh)]}))
                if h < C_HEADS - 1:
                    unit(u + 4, gx, o, hooks=({8: [turn_v(n, p + 4, 2, oh, o)]}, {8: [attend1(h, oh)]}))
                    unit(u + 5, gx, o, hooks=({}, {8: [turn_output(h, oh)]}))

            head1(0)
            with pe.Fori(0, 3) as i:
                for h in (1, 2):
                    head1(h, 2 * i)
            head1(7)
            last = C_HEADS - 1
            out_projection(U_OUT1, MID_ATT1,
                           ({8: [turn_v(HEADS - 1, U_OUT0 + 6 * C_HEADS, 2)]}, {4: [attend1(last)]},
                            {3: [turn_output(last)]}))
            feed_forward(pe, 1, U_FF1, hidden, output, output)
            stat_sum(N_FINAL)()
            stat_spread(N_FINAL)()


GX_BEFORE = {n: KT * n for n in range(N_FINAL)}


def feed_forward(eng, layer, u0, hidden, output, last_output, before_last=None):
    k0 = layer * FF_CHUNKS * KT

    def run(what, u, k, c_off, i_from, i_to):
        with eng.Fori(i_from, i_to) as i:
            for s in range(4):
                what(u + s, s, k + s, 2 * KT * c_off + 4 * i, 4 * i, KT * c_off + 4 * i, KT * c_off)

    for s in range(4):
        hidden(u0 + s, s, k0 + s)
    run(hidden, u0, k0, 0, 1, KT // 4)
    run(output, u0 + KT, k0, 0, 0, KT // 4)
    with eng.Fori(0, FF_CHUNKS - 2) as c:
        run(hidden, u0 + 2 * KT, k0 + KT, c, 0, KT // 4)
        run(output, u0 + 3 * KT, k0 + KT, c, 0, KT // 4)
    u, k = u0 + 2 * KT * (FF_CHUNKS - 1), k0 + KT * (FF_CHUNKS - 1)
    run(hidden, u, k, 0, 0, KT // 4)
    if before_last is not None:
        before_last()
    tail = 4 if layer == 1 else 0
    run(last_output, u + KT, k, 0, 0, (KT - tail) // 4)
    for s in range(KT - tail, KT):
        last_output(u + KT + s, s, k + s)


def stream_units(w_in, w_out0, ff1, ff2, w_qkv, w_out1):
    def tiles(w):
        return w.reshape(w.shape[0] // P, P, w.shape[1] // P, P).transpose(2, 1, 0, 3)

    def by_halves(w):
        t = tiles(w)
        a, b = t[0], t[1]
        h = KT // 2
        pair = np.stack([np.concatenate([a[:, :h], b[:, :h]], axis=1), np.concatenate([a[:, h:], b[:, h:]], axis=1)])
        return np.concatenate([pair, t[2:]])

    def mlp(w1, w2):
        up, down = tiles(w1), tiles(w2)
        parts = []
        for c in range(FF_CHUNKS):
            parts += [up[c * KT:(c + 1) * KT], down[:, :, c * KT:(c + 1) * KT]]
        return parts

    t = tiles(w_in)
    order0 = [x for h in range(A_HEADS) for x in (h, A_HEADS + h, 2 * A_HEADS + h)]
    order0 += [3 * A_HEADS + g for g in range(GROUPS)]
    q = tiles(w_qkv)
    n = 2 * C_HEADS
    order1 = [x for h in range(C_HEADS)
              for x in (2 * h, n + 2 * h, 2 * h + 1, n + 2 * h + 1, 2 * n + 2 * h, 2 * n + 2 * h + 1)]
    parts = [t[order0], by_halves(w_out0), *mlp(ff1[0], ff2[0]), q[order1], by_halves(w_out1), *mlp(ff1[1], ff2[1])]
    return np.concatenate(parts).reshape(UNITS, P, KT * P)


def shape_constants():
    d = np.arange(-(SEQ - 1), SEQ)
    n = np.abs(d)
    max_exact = BUCKETS // 4
    large = max_exact + (np.log(np.maximum(n, 1).astype(np.float32) / np.float32(max_exact)).astype(np.float32)
                         / np.float32(math.log(1024 / max_exact)) * np.float32(BUCKETS // 2 - max_exact)
                         ).astype(np.int32)
    bucket = np.where(d > 0, BUCKETS // 2, 0) + np.where(n < max_exact, n, np.minimum(large, BUCKETS // 2 - 1))
    onehot = np.zeros((BUCKETS + 1, LINE), np.float32)
    onehot[bucket, np.arange(d.size)] = 1.0
    reach = sum(((n % dil == 0) & (n <= window // 2)).astype(int) for window, dil in ((128, 1), (512, 4), (2048, 16)))
    onehot[BUCKETS, :d.size] = np.where(reach > 0, np.log(np.maximum(reach, 1)), -1e30)
    a_head_row = np.zeros((1, HEADS), np.float32)
    a_head_row[0, :A_HEADS] = 1.0
    c = np.arange(P)
    angle = 2 * np.pi * (np.outer(c, c) % P) / P
    channel = np.stack([np.cos(angle), np.sin(angle)], axis=1).astype(np.float32)
    s = np.arange(SEQ)
    angle = (2 * np.pi * (np.outer(s, s) % SEQ) / SEQ).reshape(QT, P, SEQ).transpose(1, 0, 2)
    position = (np.stack([np.cos(angle), -np.sin(angle)], axis=2) / math.sqrt(SEQ * P)).astype(np.float32)
    return onehot, a_head_row, channel, position, np.eye(P, dtype=np.float32)


def kernel(x, norm_mix_g, norm_ffn_g, norm_final_g, rel_bias_table, w_in_even, w_fnet, w_out_even, w_qkv_odd,
           lambda_q1, lambda_k1, lambda_q2, lambda_k2, subln_g, w_out_odd, w_ff1, w_ff2):
    import concourse.bacc as bacc
    from concourse.bass_utils import run_bass_kernel_spmd

    onehot, a_head_row, channel, position, identity = shape_constants()
    gains = np.stack([norm_mix_g[0], norm_ffn_g[0], norm_mix_g[1], norm_ffn_g[1], norm_final_g])
    arrays = {
        "xT": np.ascontiguousarray(np.asarray(x)[0].T),
        "weights": stream_units(*(np.asarray(a) for a in (w_in_even[0], w_out_even[0], w_ff1, w_ff2, w_qkv_odd[0],
                                                          w_out_odd[0]))),
        "gains": np.ascontiguousarray(gains.reshape(5, KT, P).transpose(2, 0, 1)),
        "subln": np.ascontiguousarray(np.asarray(subln_g)[0].reshape(2, P).T),
        "lambdas": np.ascontiguousarray(np.concatenate([lambda_q1, lambda_k1, lambda_q2, lambda_k2]).T),
        "table": np.ascontiguousarray(rel_bias_table),
        "w_fnet": np.ascontiguousarray(np.asarray(w_fnet)[0]),
        "onehot": onehot, "a_head_row": a_head_row, "channel_dft": channel, "position_dft": position,
        "identity": identity,
    }
    nc = bacc.Bacc("TRN2", target_bir_lowering=False, num_devices=1)
    aps = {name: nc.dram_tensor(f"{name}_dram", a.shape, mybir.dt.from_np(a.dtype), kind="ExternalInput").ap()
           for name, a in arrays.items()}
    out = nc.dram_tensor("out_dram", (D, SEQ), F32, kind="ExternalOutput").ap()
    trunk(nc, outT=out, **aps)
    result = run_bass_kernel_spmd(nc, [{f"{name}_dram": a for name, a in arrays.items()}], core_ids=[0])
    return np.ascontiguousarray(result.results[0]["out_dram"].T)[None]
```
